# Optimizing a Trainium2 kernel written in Bass

```python
import jax, jax.numpy as jnp
from jax import lax
import numpy as np

D_MODEL = 1024
BATCH = 1
SEQ = 256
DEPTH = 2

RET_HEADS = 4
RET_DK = 64
RET_DV = 128
FOX_HEADS = 4
FOX_DH = 64
MEM_HEADS = 4
MEM_DH = 64
MEM_LEN = 256
D_MIX = RET_HEADS * RET_DV + FOX_HEADS * FOX_DH + MEM_HEADS * MEM_DH
RET_CHUNK = 128
Q_BLOCK = 128
D_FF = 2752
N_EXPERTS = 8
TOP_K = 2
ROPE_BASE = 10000.0
EPS = 1e-6
N_DENSE = (DEPTH + 1) // 2
N_MOE = DEPTH // 2
IN_SPLIT = (RET_HEADS * RET_DK, RET_HEADS * RET_DK, RET_HEADS * RET_DV, RET_HEADS * RET_DV,
            FOX_HEADS * FOX_DH, FOX_HEADS * FOX_DH, FOX_HEADS * FOX_DH, FOX_HEADS,
            MEM_HEADS * MEM_DH)
IN_COLS = sum(IN_SPLIT)

kernel_name = "hybrid_retention_fox_memory_moe_trunk"

def rms_norm(x, g):
    xf = x.astype(jnp.float32)
    y = xf * lax.rsqrt(jnp.mean(xf * xf, axis=-1, keepdims=True) + EPS)
    return (y * g.astype(jnp.float32)).astype(x.dtype)

def rope(x, pos):
    half = x.shape[-1] // 2
    inv_freq = ROPE_BASE ** (-jnp.arange(half, dtype=jnp.float32) / half)
    ang = pos[:, None] * inv_freq[None, :]
    cos = jnp.cos(ang)[:, None, :]
    sin = jnp.sin(ang)[:, None, :]
    xf = x.astype(jnp.float32)
    x1, x2 = xf[..., :half], xf[..., half:]
    return jnp.concatenate([x1 * cos - x2 * sin, x2 * cos + x1 * sin], axis=-1).astype(x.dtype)

def retention(q, k, v):
    B, S, H, dk = q.shape
    dv = v.shape[-1]
    C = RET_CHUNK
    N = S // C
    log_g = jnp.log(1.0 - 2.0 ** (-5.0 - jnp.arange(H, dtype=jnp.float32)))

    def chunks(t):
        return t.astype(jnp.float32).reshape(B, N, C, H, t.shape[-1]).transpose(0, 3, 1, 2, 4)

    qc = chunks(q) * (dk ** -0.5)
    kc = chunks(k)
    vc = chunks(v)
    idx = jnp.arange(C, dtype=jnp.float32)
    diff = idx[:, None] - idx[None, :]
    dmat = jnp.where(diff >= 0, jnp.exp(log_g[:, None, None] * jnp.maximum(diff, 0.0)), 0.0)
    scores = jnp.einsum('bhnid,bhnjd->bhnij', qc, kc) * dmat[None, :, None]
    intra = jnp.einsum('bhnij,bhnje->bhnie', scores, vc)
    k_decay = jnp.exp(log_g[:, None] * (C - 1.0 - idx))
    kv = jnp.einsum('bhncd,bhnce->bhnde', kc * k_decay[None, :, None, :, None], vc)
    chunk_decay = jnp.exp(log_g * C)[None, :, None, None]

    def step(state, kv_n):
        return state * chunk_decay + kv_n, state

    _, prev = lax.scan(step, jnp.zeros((B, H, dk, dv), jnp.float32), jnp.moveaxis(kv, 2, 0))
    prev = jnp.moveaxis(prev, 0, 2)
    q_decay = jnp.exp(log_g[:, None] * (idx + 1.0))
    cross = jnp.einsum('bhncd,bhnde->bhnce', qc * q_decay[None, :, None, :, None], prev)
    out = intra + cross
    return out.transpose(0, 2, 3, 1, 4).reshape(B, S, H, dv)

def forgetting_attention(q, k, v, log_f):
    B, S, H, d = q.shape
    NB = S // Q_BLOCK
    scale = d ** -0.5
    c = lax.cumsum(log_f, axis=1).transpose(0, 2, 1)
    qh = q.transpose(0, 2, 1, 3)
    kh = k.transpose(0, 2, 1, 3)
    vh = v.transpose(0, 2, 1, 3)
    q_blocks = qh.reshape(B, H, NB, Q_BLOCK, d).transpose(2, 0, 1, 3, 4)
    c_blocks = c.reshape(B, H, NB, Q_BLOCK).transpose(2, 0, 1, 3)
    k_pos = jnp.arange(S)

    def block(args):
        qb, cb, i = args
        s = jnp.einsum('bhqd,bhkd->bhqk', qb, kh).astype(jnp.float32) * scale
        s = s + (cb[..., :, None] - c[:, :, None, :])
        q_pos = i * Q_BLOCK + jnp.arange(Q_BLOCK)
        s = jnp.where(k_pos[None, :] <= q_pos[:, None], s, -jnp.inf)
        p = jax.nn.softmax(s, axis=-1)
        return jnp.einsum('bhqk,bhkd->bhqd', p.astype(vh.dtype), vh)

    out = lax.map(block, (q_blocks, c_blocks, jnp.arange(NB)))
    return out.transpose(1, 0, 3, 2, 4).reshape(B, S, H, d)

def memory_attention(q, mk, mv):
    d = q.shape[-1]
    s = jnp.einsum('bshd,bmhd->bhsm', q, mk).astype(jnp.float32) * (d ** -0.5)
    p = jax.nn.softmax(s, axis=-1)
    return jnp.einsum('bhsm,bmhd->bshd', p.astype(mv.dtype), mv)

def hybrid_mixer(h, mem, w_in, forget_bias, fox_q_g, fox_k_g, mem_q_g, mem_k_g,
                 mem_norm_g, w_mem_kv, out_norm_g, w_out):
    B, S, _ = h.shape
    M = mem.shape[1]
    pos = jnp.arange(S, dtype=jnp.float32)
    proj = h @ w_in
    cuts = tuple(int(i) for i in np.cumsum(IN_SPLIT)[:-1])
    rq, rk, rv, rg, fq, fk, fv, ff, mq = jnp.split(proj, cuts, axis=-1)

    rq = rope(rq.reshape(B, S, RET_HEADS, RET_DK), pos)
    rk = rope(rk.reshape(B, S, RET_HEADS, RET_DK), pos)
    ret = retention(rq, rk, rv.reshape(B, S, RET_HEADS, RET_DV))

    fq = rms_norm(fq.reshape(B, S, FOX_HEADS, FOX_DH), fox_q_g)
    fk = rms_norm(fk.reshape(B, S, FOX_HEADS, FOX_DH), fox_k_g)
    log_f = jax.nn.log_sigmoid((ff + forget_bias).astype(jnp.float32))
    fox = forgetting_attention(fq, fk, fv.reshape(B, S, FOX_HEADS, FOX_DH), log_f)

    mkv = rms_norm(mem, mem_norm_g) @ w_mem_kv
    mk, mv = jnp.split(mkv, 2, axis=-1)
    mk = rms_norm(mk.reshape(B, M, MEM_HEADS, MEM_DH), mem_k_g)
    mv = mv.reshape(B, M, MEM_HEADS, MEM_DH)
    mq = rms_norm(mq.reshape(B, S, MEM_HEADS, MEM_DH), mem_q_g)
    memo = memory_attention(mq, mk, mv)

    g_ret, g_fox, g_mem = jnp.split(out_norm_g, (RET_HEADS * RET_DV, RET_HEADS * RET_DV + FOX_HEADS * FOX_DH))
    ret_o = rms_norm(ret.astype(h.dtype), g_ret.reshape(RET_HEADS, RET_DV)).reshape(B, S, -1) * jax.nn.silu(rg)
    fox_o = rms_norm(fox, g_fox.reshape(FOX_HEADS, FOX_DH)).reshape(B, S, -1)
    mem_o = rms_norm(memo, g_mem.reshape(MEM_HEADS, MEM_DH)).reshape(B, S, -1)
    y = jnp.concatenate([ret_o, fox_o.astype(ret_o.dtype), mem_o.astype(ret_o.dtype)], axis=-1)
    return (y @ w_out).astype(h.dtype)

def swiglu(h, w_gate, w_up, w_down):
    return (jax.nn.silu(h @ w_gate) * (h @ w_up)) @ w_down

def moe_ffn(h, router_w, wg, wu, wd):
    B, S, D = h.shape
    t = h.reshape(B * S, D)
    logits = (t @ router_w).astype(jnp.float32)
    top_vals, top_idx = lax.top_k(logits, TOP_K)
    gates = jax.nn.softmax(top_vals, axis=-1)
    combine = jnp.sum(jax.nn.one_hot(top_idx, N_EXPERTS, dtype=jnp.float32) * gates[..., None], axis=1)
    y = jnp.zeros((B * S, D), jnp.float32)
    for e in range(N_EXPERTS):
        y = y + combine[:, e:e + 1] * swiglu(t, wg[e], wu[e], wd[e]).astype(jnp.float32)
    return y.astype(h.dtype).reshape(B, S, D)

def setup_inputs(seed: int = 0) -> dict:
    key = jax.random.key(seed)
    ks = jax.random.split(key, 22)
    f32 = jnp.float32

    def w(k, shape, fan_in):
        return jax.random.normal(k, shape, f32) * (fan_in ** -0.5)

    def gain(k, shape):
        return 1.0 + 0.02 * jax.random.normal(k, shape, f32)

    return {
        "x": jax.random.normal(ks[0], (BATCH, SEQ, D_MODEL), f32),
        "mem": jax.random.normal(ks[1], (BATCH, MEM_LEN, D_MODEL), f32),
        "attn_norm_g": gain(ks[2], (DEPTH, D_MODEL)),
        "w_in": w(ks[3], (DEPTH, D_MODEL, IN_COLS), D_MODEL),
        "forget_bias": jax.random.uniform(ks[4], (DEPTH, FOX_HEADS), f32, minval=1.0, maxval=3.0),
        "fox_q_norm_g": gain(ks[5], (DEPTH, FOX_DH)),
        "fox_k_norm_g": gain(ks[6], (DEPTH, FOX_DH)),
        "mem_q_norm_g": gain(ks[7], (DEPTH, MEM_DH)),
        "mem_k_norm_g": gain(ks[8], (DEPTH, MEM_DH)),
        "mem_norm_g": gain(ks[9], (DEPTH, D_MODEL)),
        "w_mem_kv": w(ks[10], (DEPTH, D_MODEL, 2 * MEM_HEADS * MEM_DH), D_MODEL),
        "out_norm_g": gain(ks[11], (DEPTH, D_MIX)),
        "w_out": w(ks[12], (DEPTH, D_MIX, D_MODEL), D_MIX),
        "ffn_norm_g": gain(ks[13], (DEPTH, D_MODEL)),
        "dense_w_gate": w(ks[14], (N_DENSE, D_MODEL, D_FF), D_MODEL),
        "dense_w_up": w(ks[15], (N_DENSE, D_MODEL, D_FF), D_MODEL),
        "dense_w_down": w(ks[16], (N_DENSE, D_FF, D_MODEL), D_FF),
        "router_w": w(ks[17], (N_MOE, D_MODEL, N_EXPERTS), D_MODEL),
        "expert_w_gate": w(ks[18], (N_MOE, N_EXPERTS, D_MODEL, D_FF), D_MODEL),
        "expert_w_up": w(ks[19], (N_MOE, N_EXPERTS, D_MODEL, D_FF), D_MODEL),
        "expert_w_down": w(ks[20], (N_MOE, N_EXPERTS, D_FF, D_MODEL), D_FF),
    }

def reference(x, mem, attn_norm_g, w_in, forget_bias, fox_q_norm_g, fox_k_norm_g, mem_q_norm_g,
              mem_k_norm_g, mem_norm_g, w_mem_kv, out_norm_g, w_out, ffn_norm_g, dense_w_gate,
              dense_w_up, dense_w_down, router_w, expert_w_gate, expert_w_up, expert_w_down):
    for l in range(DEPTH):
        h = rms_norm(x, attn_norm_g[l])
        x = x + hybrid_mixer(h, mem, w_in[l], forget_bias[l], fox_q_norm_g[l], fox_k_norm_g[l],
                             mem_q_norm_g[l], mem_k_norm_g[l], mem_norm_g[l], w_mem_kv[l],
                             out_norm_g[l], w_out[l])
        h = rms_norm(x, ffn_norm_g[l])
        j = l // 2
        if l % 2 == 0:
            x = x + swiglu(h, dense_w_gate[j], dense_w_up[j], dense_w_down[j])
        else:
            x = x + moe_ffn(h, router_w[j], expert_w_gate[j], expert_w_up[j], expert_w_down[j])
    return x


_drawn_inputs = setup_inputs


def setup_inputs(seed=0):
    import zlib

    import numpy as np

    out = dict(_drawn_inputs(seed))
    spreads = {}
    factors = {'fox_k_norm_g': 4.857, 'mem_k_norm_g': 2.827}
    for name, (base, spread) in spreads.items():
        noise = np.random.default_rng([zlib.crc32(name.encode()), seed]).standard_normal(out[name].shape)
        drawn = base * np.exp(spread * noise) if base else spread * noise
        out[name] = __import__('jax').numpy.asarray(drawn.astype(out[name].dtype))
    for name, factor in factors.items():
        out[name] = (out[name] * factor).astype(out[name].dtype)
    return out
```

```python
from contextlib import ExitStack

import numpy as np
import concourse.bass as bass
from concourse import mybir

F32 = mybir.dt.float32
F32R = mybir.dt.float32r
BF16 = mybir.dt.bfloat16
I32 = mybir.dt.int32
U32 = mybir.dt.uint32
ACT = mybir.ActivationFunctionType
ALU = mybir.AluOpType
AX = mybir.AxisListType

P = 128
SEQ, D = 256, 1024
NB = SEQ // P
KT = D // P
DEPTH = 2
RH, RDV = 4, 128
DH = 64
H = 4
QK = H * DH
EPS = 1e-6
SCALE = DH ** -0.5
D_FF = 2752
E_ = 8
W = 512
LAST = D_FF - (D_FF // W - 1) * W
CH = [W] * (D_FF // W - 1) + [-(-LAST // 256) * 128, LAST - -(-LAST // 256) * 128]
C0 = [sum(CH[:c]) for c in range(len(CH))]
assert all(256 < n <= W for n in CH)
NCH = len(CH)
RAW, SPLIT = 9, 3
SLOT = 2080
LPC = 6
assert (LPC * NCH) % RAW == 0 and RAW % SPLIT == 0
NEG = -1e30

RQ, RV, RG, FQ, FV, FF, MQ = 0, 512, 1024, 1536, 2048, 2304, 2308

G_ATT, G_FFN, G_OUT, G_MEM = 0, 16, 32, 48
G_FQ, G_FK, G_MQ, G_MK = 64, 66, 68, 70
BIAS, ROUT = 72, 80
NPAR = ROUT + KT * E_
T_DEC = 0
T_COS = T_DEC + 4 * SEQ
T_SIN = T_COS + NB * 32
T_ID = T_SIN + NB * 32
T_TRI = T_ID + P
T_ONE = T_TRI + P
T_MASK = T_ONE + P
T_IOTA = T_MASK + P
NTAB = T_IOTA + P

AR_AUG, AR_FV, AR_RQK, AR_RV = 0, 1056, 1568, 2592
AR_FT, AR_MQT, AR_PF, AR_PT = 3616, 5664, 6176, 8224
NAR = AR_PT + 1536
HEAD_AT = [0, 2, 1, 3]


def loads_of_trunk():
    out = [("kv", l, h) for l in range(DEPTH) for h in range(2)]
    for l in range(DEPTH):
        out += [("in", l, FQ, W, h) for h in range(2)]
        out += [("in", l, FV, QK + H, None), ("in", l, MQ, QK, None)]
        out += [("in", l, c, W, h) for c in (RQ, RV, RG) for h in range(2)]
        out += [("out", l, h) for h in range(4)]
        if l == 0:
            for c in range(NCH):
                out += [("gate", c, h) for h in range(2)]
                if c:
                    out += [("down", c - 1, h) for h in range(2)]
                out += [("up", c, h) for h in range(2)]
            out += [("down", NCH - 1, h) for h in range(2)]
    return out


LOADS = loads_of_trunk()
MOE0 = len(LOADS)
MOE_LOADS = E_ * NCH * LPC
LAYER_LOADS = 14
KV0, IN0 = 0, 4
DENSE0 = IN0 + LAYER_LOADS
IN1 = DENSE0 + NCH * LPC


def build(nc, x, mem, w_in, w_mem_kv, w_out, dwg, dwu, dwd, ewg, ewu, ewd, par, tab, out):
    with ExitStack() as ctx:
        def sb(name, shape, dt=F32):
            return ctx.enter_context(nc.sbuf_tensor(name, shape, dt))

        sems = {}

        def sem(name):
            if name not in sems:
                sems[name] = ctx.enter_context(nc.semaphore("s_" + name))
            return sems[name]

        raw = sb("raw", [P, RAW, SLOT])
        whi = sb("whi", [P, SPLIT, SLOT], F32R)
        wlo = sb("wlo", [P, SPLIT, SLOT], F32R)
        xres = sb("xres", [P, NB, D])
        tok = sb("tok", [P, NB, D])
        sthi = sb("sthi", [P, NB, KT, P], F32R)
        stlo = sb("stlo", [P, NB, KT, P], F32R)
        hidhi = sb("hidhi", [P, NB, 4, P], F32R)
        hidlo = sb("hidlo", [P, NB, 4, P], F32R)
        scaled = sb("scaled", [P, 2, W])
        mkT = sb("mkT", [P, DEPTH, 2, SEQ])
        mval = sb("mval", [P, DEPTH, NB, QK])
        prm = sb("prm", [P, NPAR])
        tb = sb("tb", [P, NTAB])
        rthi = sb("rthi", [P, KT, E_], F32R)
        rtlo = sb("rtlo", [P, KT, E_], F32R)
        st = sb("st", [P, 128])
        guess = sb("guess", [P, 16], I32)
        newton = sb("newton", [P, 16])
        idb = sb("idb", [P, P], BF16)
        maskb = sb("maskb", [P, P], BF16)
        sel = sb("sel", [P, NB, E_])
        comb = sb("comb", [P, NB, E_])
        slot_of = sb("slot_of", [P, NB, 2 * E_ + 1])
        mx = sb("mx", [P, NB, 8])
        mi = sb("mi", [P, NB, 8], U32)
        mif = sb("mif", [P, NB, 8])
        flag = sb("flag", [P, 1], I32)
        ps = ctx.enter_context(nc.psum_tensor("ps", [P, 8, W], F32))

        with nc.sbuf_tensor("arena", [P, NAR], F32) as arena:
            pass
        sil = sb("sil", [P, NB, W])
        hid = sb("hid", [P, NB, W])
        onehot = sb("onehot", [P, NB, P], F32R)
        onehotT = sb("onehotT", [P, 2, NB, P], F32R)
        outhi, outlo = (sb(f"out{part_}", [P, D], F32R) for part_ in ("hi", "lo"))
        tokhi, toklo = (sb(f"tok{part_}", [P, NB, D], F32R) for part_ in ("hi", "lo"))

        ident = tb[:, T_ID:T_ID + P]
        tri = tb[:, T_TRI:T_TRI + P]
        ones = tb[:, T_ONE:T_ONE + P]
        decay = tb[:, T_DEC:T_DEC + 4 * SEQ].rearrange("p (h i) -> p h i", h=4)
        cos = tb[:, T_COS:T_COS + NB * 32].rearrange("p (b i) -> p b i", b=NB)
        sin = tb[:, T_SIN:T_SIN + NB * 32].rearrange("p (b i) -> p b i", b=NB)

        def ar(at, n):
            return arena[:, at:at + n]

        aug = ar(AR_AUG, 1056).rearrange("p (b h d) -> p b h d", b=NB, h=2 * H)
        fval = ar(AR_FV, 512).rearrange("p (b d) -> p b d", b=NB)
        rqk = ar(AR_RQK, 1024).rearrange("p (b d) -> p b d", b=NB)
        rval = ar(AR_RV, 1024).rearrange("p (b d) -> p b d", b=NB)
        fT = ar(AR_FT, 2048).rearrange("p (h t) -> p h t", h=2 * H)
        mqT = ar(AR_MQT, 512).rearrange("p (c t) -> p c t", c=2)
        rT = ar(AR_AUG, 1024).rearrange("p (c t) -> p c t", c=4)
        pf0 = ar(AR_PF, 512).rearrange("p (h t) -> p h t", h=4)
        pf1 = ar(AR_PF + 512, 1024).rearrange("p (h t) -> p h t", h=4)
        fpT0 = ar(AR_PT, 512).rearrange("p (h t) -> p h t", h=4)
        fpT1 = ar(AR_PT + 512, 1024).rearrange("p (h t) -> p h t", h=8)
        pm = [ar(AR_PF + 1024 * b, 1024).rearrange("p (h t) -> p h t", h=4) for b in range(NB)]
        mpT = [ar(AR_FT + 1024 * b, 1024).rearrange("p (h t) -> p h t", h=8) for b in range(NB)]
        rpT0 = ar(AR_PT, 1024).rearrange("p (h t) -> p h t", h=4)
        rpT1 = ar(AR_PT + 1024, 512).rearrange("p (h t) -> p h t", h=4)
        sq_early = ar(AR_PF, 1024).rearrange("p (b d) -> p b d", b=NB)
        logf = st[:, 64:72].rearrange("p (b h) -> p b h", b=NB)
        yret = tok[:, :, 0:512]
        yfox = tok[:, :, 512:768]
        ymem = tok[:, :, 768:1024]

        block = ctx.enter_context(nc.Block())

        def views(n):
            kind = LOADS[n]
            k, cols = {"kv": (4, W), "out": (2, D)}.get(kind[0], (None, None))
            if kind[0] == "in":
                k, cols = (8, kind[3]) if kind[4] is None else (4, W)
            return k, cols

        def part(t, slot, k, cols, rows=P):
            return t[0:rows, slot, 0:k * cols].rearrange("p (k n) -> p k n", k=k)

        def ffn_shape(kind, c, h):
            if kind != "down":
                return P, 4, CH[c]
            rest = 2 * P if h == 0 else CH[c] - 2 * P
            return min(P, rest), max(1, rest // P), D

        def ffn_source(wg, wu, wd, kind, c, h):
            if kind == "down":
                rows, k, _ = ffn_shape(kind, c, h)
                r0 = C0[c] + h * 2 * P
                return wd[r0:r0 + rows * k, :].rearrange("(k p) n -> p k n", p=rows)
            w = wg if kind == "gate" else wu
            return w[h * 512:(h + 1) * 512, C0[c]:C0[c] + CH[c]].rearrange("(k p) n -> p k n", p=P)

        def shape_of(n):
            if LOADS[n][0] in ("gate", "up", "down"):
                return ffn_shape(*LOADS[n])
            return (P, *views(n))

        def source_of(n):
            kind = LOADS[n]
            if kind[0] == "kv":
                return w_mem_kv[kind[1], kind[2] * 512:(kind[2] + 1) * 512, :].rearrange("(k p) n -> p k n", p=P)
            if kind[0] == "out":
                return w_out[kind[1], kind[2] * 256:(kind[2] + 1) * 256, :].rearrange("(k p) n -> p k n", p=P)
            if kind[0] == "in":
                _, l, c, n_, h = kind
                r0, r1 = (0, D) if h is None else (h * 512, (h + 1) * 512)
                return w_in[l, r0:r1, c:c + n_].rearrange("(k p) n -> p k n", p=P)
            return ffn_source(dwg[0], dwu[0], dwd[0], *kind)

        def moe_order(first):
            return [("gate", 0), ("gate", 1), ("up", 0), ("up", 1)] + ([] if first else [("down", 0), ("down", 1)])

        PAIR = 2 * NCH * LPC

        def first_of(it, par, c):
            return isinstance(it, int) and par == 0 and c == 0

        def moe_number(rnd, it, par, c, j):
            base = MOE0 + rnd * MOE_LOADS + par * NCH * LPC + c * LPC + j
            return base if first_of(it, par, c) else base - 2

        def counted(n, it, per=PAIR):
            return it * per + n

        def landed(eng, n, it=0):
            eng.wait_ge(sem(f"landed{n % RAW}"), counted(16 * (n // RAW + 1), it, PAIR // RAW * 16))

        def used(eng, n, it=0):
            eng.wait_ge(sem("weights_used"), counted(n + 1, it))

        def split_hi(eng, n, shape, it=0):
            landed(eng, n, it)
            if n >= SPLIT:
                used(eng, n - SPLIT, it)
            rows, k, cols = shape
            eng.activation(whi[0:rows, n % SPLIT, 0:k * cols], raw[0:rows, n % RAW, 0:k * cols],
                           ACT.Copy).then_inc(sem("hi_ready"), 1)

        def split_lo(eng, n, shape, it=0):
            eng.wait_ge(sem("hi_ready"), counted(n + 1, it))
            rows, k, cols = shape
            eng.tensor_tensor(wlo[0:rows, n % SPLIT, 0:k * cols], raw[0:rows, n % RAW, 0:k * cols],
                              whi[0:rows, n % SPLIT, 0:k * cols].bitcast(F32), ALU.subtract)\
                .then_inc(sem("lo_ready"), 1)

        def fetch(eng, n, src, shape, it=0):
            rows, k, cols = shape
            if n >= RAW:
                eng.wait_ge(sem("lo_ready"), counted(n - RAW + 1, it))
            eng.dma_start(part(raw, n % RAW, k, cols, rows), src).then_inc(sem(f"landed{n % RAW}"), 16)

        def ahead(split, eng, n):
            if n + SPLIT < MOE0 + SPLIT:
                split(eng, n + SPLIT, shape_of(n + SPLIT) if n + SPLIT < MOE0 else (P, 4, W))

        def moe_stages(rnd, it):
            out = []
            for par in range(2):
                for c in range(NCH):
                    for j, (kind, h) in enumerate(moe_order(first_of(it, par, c))):
                        out.append((par, c, j, moe_number(rnd, it, par, c, j),
                                    ffn_shape(kind, (c - 1) % NCH if kind == "down" else c, h)))
            return out

        def split_pair(split, eng, rnd, it, after):
            loads = moe_stages(rnd, it)
            if not (isinstance(it, int) and rnd == 0):
                for _, _, _, n, shape in loads[:SPLIT]:
                    split(eng, n, shape, it)
            for i, (par, c, j, n, _) in enumerate(loads):
                if i + SPLIT < len(loads):
                    split(eng, loads[i + SPLIT][3], loads[i + SPLIT][4], it)
                after(par, c, moe_order(first_of(it, par, c))[j], n)

        FLUSH = [ffn_shape("down", NCH - 1, h) for h in range(2)]

        TURNS = {"mem0": 0, "mem1": 1, "att0": 2, "out0": 3, "ffn0": 4, "att1": 5, "out1": 6, "ffn1": 7}
        ROWS = {"mem0": 0, "mem1": 0, "att0": 1, "out0": 2, "ffn0": 3, "att1": 4, "out1": 5, "ffn1": 6}
        GAIN = {"mem0": G_MEM, "mem1": G_MEM + KT, "att0": G_ATT, "att1": G_ATT + KT, "out0": G_OUT,
                "out1": G_OUT + KT, "ffn0": G_FFN, "ffn1": G_FFN + KT}
        SQ = {"mk0": 0, "mk1": 1}
        for l in range(DEPTH):
            SQ.update({f"{w}{l}": 2 + 5 * l + i for i, w in enumerate(("fqk", "mq", "fo", "ro", "mo"))})
        DENSE_UNITS = NB * NCH

        @block.sync
        def _(sp):
            sp.dma_start(tb[:, :], tab).then_inc(sem("tables"), 16)
            sp.dma_start(prm[:, :], par).then_inc(sem("params"), 16)
            sp.dma_start(tok[:, :, :], mem[0].rearrange("(b p) d -> p b d", p=P)).then_inc(sem("mem_in"), 16)
            sp.dma_start(xres[:, :, :], x[0].rearrange("(b p) d -> p b d", p=P)).then_inc(sem("x_in"), 16)
            for n in range(MOE0):
                fetch(sp, n, source_of(n), shape_of(n))

            def fetch_pair(rnd, it):
                for par in range(2):
                    for c in range(NCH):
                        for j, (kind, h) in enumerate(moe_order(first_of(it, par, c))):
                            cc = c - 1 if kind == "down" else c
                            e = it * 2 + par - (1 if cc < 0 else 0)
                            cc %= NCH
                            fetch(sp, moe_number(rnd, it, par, c, j),
                                  ffn_source(expert(ewg, e), expert(ewu, e), expert(ewd, e), kind, cc, h),
                                  ffn_shape(kind, cc, h), it)

            def expert(w, e):
                if isinstance(e, int):
                    return w[0, e]
                return w[0, bass.ds(e, 1)].rearrange("a r n -> (a r) n")

            def fetch_round(rnd):
                fetch_pair(rnd, 0)
                with sp.Fori(1, E_ // 2) as it:
                    fetch_pair(rnd, it)
                for h in range(2):
                    fetch(sp, MOE0 + (rnd + 1) * MOE_LOADS - 2 + h,
                          ffn_source(None, None, ewd[0, E_ - 1], "down", NCH - 1, h), FLUSH[h])

            fetch_round(0)
            sp.wait_ge(sem("flag_ready"), 1)
            with sp.If(sp.value_load(flag[0:1, 0:1], min_val=0, max_val=1) > 0):
                fetch_round(1)
            with sp.Else():
                sp.nop()
            sp.wait_ge(sem("x_final"), 1)
            sp.dma_start(out[0].rearrange("(b p) d -> p b d", p=P), xres[:, :, :]).then_inc(sem("stored"), 16)
            sp.wait_ge(sem("stored"), 16)

        @block.tensor
        def _(pe):
            def product(dst, rows, lhs, n, k, nk, cols, c0, c1, start, stop):
                xh, xl = lhs
                wh = part(whi, n % SPLIT, nk, cols, rows)[:, k, c0:c1]
                wl = part(wlo, n % SPLIT, nk, cols, rows)[:, k, c0:c1]
                pe.matmul(dst, xh, wh, start=start, stop=False)
                pe.matmul(dst, xh, wl, start=False, stop=False)
                return pe.matmul(dst, xl, wh, start=False, stop=stop)

            def stat(b, k):
                return sthi[:, b, k, :], stlo[:, b, k, :]

            def turn(name):
                for u in range(4):
                    b, half = u // 2, u % 2
                    g = 4 * TURNS[name] + u
                    pe.wait_ge(sem("rows_ready"), NB * ROWS[name] + b + 1)
                    if g >= 2:
                        pe.wait_ge(sem("turn_scaled"), g - 1)
                    for k in range(4):
                        d0 = (half * 4 + k) * P
                        last = pe.transpose(ps[:, 4 + g % 2, k * P:(k + 1) * P], tok[:, b, d0:d0 + P], ident)
                    last.then_inc(sem("turned"), 1)
                pe.wait_ge(sem("turn_lo"), 4 * (TURNS[name] + 1))

            def project(n, bank, cols, halves):
                nk = KT // halves
                for h in range(halves):
                    pe.wait_ge(sem("lo_ready"), n + h + 1)
                    for b in range(NB):
                        for k in range(nk):
                            last = product(ps[:, bank + b, 0:cols], P, stat(b, h * nk + k), n + h, k, nk, cols, 0, cols,
                                           start=(h == 0 and k == 0), stop=(h == halves - 1 and k == nk - 1))
                    last.then_inc(sem("weights_used"), 1)

            def transposes(dst, tiles):
                for i, t in enumerate(tiles):
                    last = pe.transpose(dst(i), t, ident)
                return last

            pe.wait_ge(sem("tables"), 16)
            for l in range(DEPTH):
                turn(f"mem{l}")
                project(KV0 + 2 * l, 2 * l, W, 2)
                pe.wait_ge(sem("mk_rows"), l + 1)
                if l:
                    pe.wait_ge(sem("mk_T"), l)
                transposes(lambda i: ps[:, 6, i * P:(i + 1) * P],
                           [rqk[:, b, c * P:(c + 1) * P] for c in range(2) for b in range(NB)])\
                    .then_inc(sem("mk_turned"), 1)

            def mixer(l, n):
                v = l + 1
                turn(f"att{l}")
                if l == 0:
                    pe.wait_ge(sem("mk_rows"), DEPTH)
                project(n, 0, W, 2)
                project(n + 2, 2, QK + H, 1)
                pe.wait_ge(sem("fqk_rows"), v)
                project(n + 3, 0, QK, 1)
                pe.wait_ge(sem("logf"), v)
                pe.wait_ge(sem("mk_T"), DEPTH)
                sum0, sum1 = ps[:, 6, 0:4], ps[:, 6, 4:8]
                pe.matmul(sum0, tri, logf[:, 0], start=True, stop=True)
                pe.matmul(sum1, tri, logf[:, 1], start=True, stop=False)
                pe.matmul(sum1, ones, logf[:, 0], start=False, stop=True).then_inc(sem("logf_summed"), 1)
                pe.wait_ge(sem("fv_copied"), v)
                project(n + 4, 2, W, 2)
                pe.wait_ge(sem("aug_ready"), v)
                transposes(lambda i: ps[0:66, 4 + i // 4, (i % 4) * P:(i % 4 + 1) * P],
                           [aug[:, b, h, :] for h in range(2 * H) for b in range(NB)]).then_inc(sem("f_turned"), 1)
                pe.wait_ge(sem("mq_rows"), v)
                project(n + 6, 0, W, 2)
                pe.wait_ge(sem("f_T"), 2 * v)
                pe.wait_ge(sem("mask_ready"), 2)
                for b in range(NB):
                    nk = (b + 1) * P
                    for h in range(H):
                        dst = ps[:, 4, h * P:(h + 1) * P] if b == 0 else ps[:, 5 + h // 2, (h % 2) * SEQ:(h % 2) * SEQ + nk]
                        pe.matmul(dst, fT[0:66, h, b * P:(b + 1) * P], fT[0:66, H + h, 0:nk], start=True, stop=False)
                        last = pe.matmul(dst[:, b * P:nk], idb[:, :], maskb[:, :], start=False, stop=True)
                    last.then_inc(sem("f_scored"), 1)
                transposes(lambda i: ps[:, 7, i * P:(i + 1) * P],
                           [ymem[:, b, c * P:(c + 1) * P] for c in range(2) for b in range(NB)])\
                    .then_inc(sem("mq_turned"), 1)
                pe.wait_ge(sem("r_rotated"), v)
                transposes(lambda i: ps[:, 2 + i // 4, (i % 4) * P:(i % 4 + 1) * P],
                           [rqk[:, b, c * P:(c + 1) * P] for c in range(4) for b in range(NB)])\
                    .then_inc(sem("r_turned"), 1)
                pe.wait_ge(sem("rv_copied"), v)
                project(n + 8, 0, W, 2)
                pe.wait_ge(sem("f_exp"), NB * l + 1)
                transposes(lambda i: ps[:, 4, i * P:(i + 1) * P], [pf0[:, h, :] for h in range(H)])\
                    .then_inc(sem("f_pturned"), 1)
                pe.wait_ge(sem("f_exp"), NB * l + 2)
                transposes(lambda i: ps[:, 5 + i // 4, (i % 4) * P:(i % 4 + 1) * P],
                           [pf1[:, h, j * P:(j + 1) * P] for h in range(H) for j in range(NB)])\
                    .then_inc(sem("f_pturned"), 1)

                def head_rows(h):
                    return slice(DH * (h % 2), DH * (h % 2) + DH)

                def mem_scores(b, bank):
                    for h in range(H):
                        r = head_rows(h)
                        last = pe.matmul(ps[:, bank + h % 2, (h // 2) * SEQ:(h // 2 + 1) * SEQ],
                                         mqT[r, h // 2, b * P:(b + 1) * P], mkT[r, l, h // 2, :], start=True, stop=True)
                    last.then_inc(sem("m_scored"), 1)

                pe.wait_ge(sem("r_T"), v)
                pe.wait_ge(sem("mq_T"), v)
                mem_scores(0, 2)
                pe.wait_ge(sem("f_pT"), NB * v)
                for b in range(NB):
                    for h in range(H):
                        dst = ps[:, 7, b * QK + h * DH:b * QK + (h + 1) * DH]
                        for j in range(b + 1):
                            last = pe.matmul(dst, fpT0[:, h, :] if b == 0 else fpT1[:, 2 * h + j, :],
                                             fval[:, j, h * DH:(h + 1) * DH], start=(j == 0), stop=(j == b))
                last.then_inc(sem("f_valued"), 1)
                mem_scores(1, 4)
                pe.wait_ge(sem("gate_silu"), v)
                for h in range(RH):
                    r = head_rows(h)
                    last = pe.matmul(ps[:, h % 2, (h // 2) * SEQ:(h // 2 + 1) * SEQ], rT[r, 2 + h // 2, 0:P],
                                     rT[r, h // 2, :], start=True, stop=True)
                last.then_inc(sem("r_scored"), 1)
                pe.wait_ge(sem("f_out"), v)
                for h in range(RH):
                    r = head_rows(h)
                    last = pe.matmul(ps[:, 6 + h % 2, (h // 2) * P:(h // 2 + 1) * P], rT[r, 2 + h // 2, P:SEQ],
                                     rT[r, h // 2, P:SEQ], start=True, stop=True)
                last.then_inc(sem("r_scored"), 1)
                for b in range(NB):
                    pe.wait_ge(sem("m_exp"), NB * l + b + 1)
                    transposes(lambda i: ps[:, 2 + 2 * b + i // 4, (i % 4) * P:(i % 4 + 1) * P],
                               [pm[b][:, HEAD_AT[h], j * P:(j + 1) * P] for h in range(H) for j in range(NB)])\
                        .then_inc(sem("m_pturned"), 1)
                pe.wait_ge(sem("r_decayed"), 2 * v)
                for b in range(NB):
                    for h in range(RH):
                        a = HEAD_AT[h]
                        dst = ps[:, b, h * RDV:(h + 1) * RDV]
                        last = pe.matmul(dst, rpT0[:, a, b * P:(b + 1) * P], rval[:, 0, h * RDV:(h + 1) * RDV],
                                         start=True, stop=(b == 0))
                        if b:
                            last = pe.matmul(dst, rpT1[:, a, :], rval[:, 1, h * RDV:(h + 1) * RDV], start=False, stop=True)
                last.then_inc(sem("r_valued"), 1)
                pe.wait_ge(sem("m_pT"), NB * v)
                for b in range(NB):
                    for h in range(H):
                        dst = ps[:, 6, b * QK + h * DH:b * QK + (h + 1) * DH]
                        for j in range(NB):
                            last = pe.matmul(dst, mpT[b][:, 2 * h + j, :], mval[:, l, j, h * DH:(h + 1) * DH],
                                             start=(j == 0), stop=(j == NB - 1))
                last.then_inc(sem("m_valued"), 1)
                turn(f"out{l}")
                for q in range(4):
                    m = n + 10 + q
                    pe.wait_ge(sem("lo_ready"), m + 1)
                    for b in range(NB):
                        for k in range(2):
                            for half in range(2):
                                last = product(ps[:, 2 * b + half, :], P, stat(b, 2 * q + k), m, k, 2, D,
                                               half * W, (half + 1) * W, start=(q == 0 and k == 0), stop=(q == 3 and k == 1))
                    last.then_inc(sem("weights_used"), 1)

            def widths(kind, n, it, c, h, nb, par, bank, unit):
                pe.wait_ge(sem("lo_ready"), counted(n + 1, it))
                for b in range(nb):
                    if h == 0 and unit + b >= nb:
                        pe.wait_ge(sem("silu_done" if kind == "gate" else "hidden_ready"),
                                   counted(unit + b - nb + 1, it, 2 * NCH))
                    for k in range(4):
                        last = product(ps[:, bank + b, 0:CH[c]], P, stat(b if nb > 1 else par, 4 * h + k), n, k, 4,
                                       CH[c], 0, CH[c], start=(h == 0 and k == 0), stop=(h == 1 and k == 3))
                last.then_inc(sem("weights_used"), 1)

            def turn_hidden(it, c, nb, bank, unit):
                for b in range(nb):
                    pe.wait_ge(sem("hidden_ready"), counted(unit + b + 1, it, 2 * NCH))
                    if unit + b >= nb:
                        pe.wait_ge(sem("hid_lo"), counted(unit + b - nb + 1, it, 2 * NCH))
                    for k in range(-(-CH[c] // P)):
                        f = min(P, CH[c] - k * P)
                        last = pe.transpose(ps[0:f, bank + b, k * P:(k + 1) * P], hid[:, b, k * P:k * P + f], ident)
                    last.then_inc(sem("hid_turned"), 1)

            def down(n, it, c, h, nb, unit, start, stop):
                pe.wait_ge(sem("lo_ready"), counted(n + 1, it))
                rows, nk, _ = ffn_shape("down", c, h)
                for b in range(nb):
                    if h == 0:
                        pe.wait_ge(sem("hid_lo"), counted(unit + b + 1, it, 2 * NCH))
                    for k in range(nk):
                        kk = 2 * h + k
                        for half in range(2):
                            last = product(ps[:, 4 + 2 * b + half, :], rows,
                                           (hidhi[0:rows, b, kk, :], hidlo[0:rows, b, kk, :]), n, k, nk, D,
                                           half * W, (half + 1) * W, start=(start and h == 0 and k == 0),
                                           stop=(stop and h == 1 and k == nk - 1))
                last.then_inc(sem("weights_used"), 1)

            mixer(0, IN0)
            turn("ffn0")
            n = DENSE0
            for c in range(NCH):
                widths("gate", n, 0, c, 0, NB, 0, 0, NB * c)
                if c:
                    turn_hidden(0, c - 1, NB, 2, NB * (c - 1))
                widths("gate", n + 1, 0, c, 1, NB, 0, 0, NB * c)
                n += 2
                if c:
                    for h in range(2):
                        down(n + h, 0, c - 1, h, NB, NB * (c - 1), c == 1, False)
                    n += 2
                for h in range(2):
                    widths("up", n + h, 0, c, h, NB, 0, 2, NB * c)
                n += 2
            turn_hidden(0, NCH - 1, NB, 2, NB * (NCH - 1))
            for h in range(2):
                down(n + h, 0, NCH - 1, h, NB, NB * (NCH - 1), False, True)

            mixer(1, IN1)
            turn("ffn1")
            pe.wait_ge(sem("router_lo"), 1)
            for b in range(NB):
                dst = ps[:, 6, b * E_:(b + 1) * E_]
                for k in range(KT):
                    xh, xl = stat(b, k)
                    pe.matmul(dst, xh, rthi[:, k, :], start=(k == 0), stop=False)
                    pe.matmul(dst, xh, rtlo[:, k, :], start=False, stop=False)
                    last = pe.matmul(dst, xl, rthi[:, k, :], start=False, stop=(k == KT - 1))
            last.then_inc(sem("logits"), 1)
            pe.wait_ge(sem("chosen"), 1)
            upto0, upto1, total = (ps[:, 7, i * E_:(i + 1) * E_] for i in range(3))
            pe.matmul(upto0, tri, sel[:, 0], start=True, stop=True)
            pe.matmul(upto1, tri, sel[:, 1], start=True, stop=False)
            pe.matmul(upto1, ones, sel[:, 0], start=False, stop=True)
            pe.matmul(total, ones, sel[:, 0], start=True, stop=False)
            pe.matmul(total, ones, sel[:, 1], start=False, stop=True).then_inc(sem("ranked"), 1)

            def turn_onehot(k, it):
                pe.wait_ge(sem("onehot_ready"), counted(k + 1, it, 2))
                if k:
                    pe.wait_ge(sem("gathered_scaled"), counted(2 * k, it, 4))
                transposes(lambda b: ps[:, 3, b * P:(b + 1) * P], [onehot[:, b, :].bitcast(F32) for b in range(NB)])\
                    .then_inc(sem("onehot_turned"), 1)

            def gather(k, it, half):
                if half == 0:
                    pe.wait_ge(sem("onehot_T"), counted(k + 1, it, 2))
                else:
                    pe.wait_ge(sem("gathered_scaled"), counted(2 * k + 1, it, 4))
                for t in range(4):
                    d0 = (4 * half + t) * P
                    for b in range(NB):
                        dst = ps[:, 3, t * P:(t + 1) * P]
                        pe.matmul(dst, tokhi[:, b, d0:d0 + P], onehot[:, b, :], start=(b == 0), stop=False)
                        last = pe.matmul(dst, toklo[:, b, d0:d0 + P], onehot[:, b, :], start=False, stop=(b == NB - 1))
                last.then_inc(sem("gathered"), 1)

            def scatter(k, it, par, b):
                pe.wait_ge(sem("out_copied"), counted(k + 1, it, 2))
                if 2 * k + b:
                    pe.wait_ge(sem("scatter_added"), counted(2 * k + b, it, 4))
                for half in range(2):
                    cols = slice(half * W, (half + 1) * W)
                    pe.matmul(ps[:, 6 + half, :], onehotT[:, par, b, :], outhi[:, cols], start=True, stop=False)
                    last = pe.matmul(ps[:, 6 + half, :], onehotT[:, par, b, :], outlo[:, cols], start=False, stop=True)
                last.then_inc(sem("scattered"), 1)

            def expert_pair(rnd, it):
                for par in range(2):
                    k = rnd * E_ + par
                    before = not (isinstance(it, int) and par == 0)
                    for c in range(NCH):
                        u = DENSE_UNITS + k * NCH + c
                        def at(j):
                            return moe_number(rnd, it, par, c, j)
                        if c == 0:
                            pe.wait_ge(sem("gathered_lo"), counted(2 * k + 2, it, 4))
                        for h in range(2):
                            widths("gate", at(h), it, c, h, 1, par, 0, u)
                        if c or before:
                            turn_hidden(it, (c - 1) % NCH, 1, 1, u - 1)
                        for h in range(2):
                            widths("up", at(2 + h), it, c, h, 1, par, 2, u)
                        if c == 1 and before:
                            scatter(k - 1, it, 1 - par, 0)
                        if c == 2:
                            if before:
                                scatter(k - 1, it, 1 - par, 1)
                            turn_onehot(k + 1, it)
                        if c in (3, 4):
                            gather(k + 1, it, c - 3)
                        if c == 1 and (k or not isinstance(it, int)):
                            pe.wait_ge(sem("out_copied"), counted(k, it, 2))
                        if c or before:
                            for h in range(2):
                                down(at(4 + h), it, (c - 1) % NCH, h, 1, u - 1, c == 1, c == 0)

            def expert_round(rnd):
                expert_pair(rnd, 0)
                with pe.Fori(1, E_ // 2) as it:
                    expert_pair(rnd, it)
                u = DENSE_UNITS + (rnd + 1) * E_ * NCH - 1
                turn_hidden(0, NCH - 1, 1, 1, u)
                for h in range(2):
                    down(MOE0 + (rnd + 1) * MOE_LOADS - 2 + h, 0, NCH - 1, h, 1, u, False, True)
                for b in range(NB):
                    scatter((rnd + 1) * E_ - 1, 0, 1, b)

            turn_onehot(0, 0)
            pe.wait_ge(sem("rows_split"), 1)
            for half in range(2):
                gather(0, 0, half)
            expert_round(0)
            pe.wait_ge(sem("flag_ready"), 1)
            with pe.If(pe.value_load(flag[0:1, 0:1], min_val=0, max_val=1) > 0):
                expert_round(1)
            with pe.Else():
                pe.nop()

        @block.scalar
        def _(act):
            own = [0]

            def then(ins):
                own[0] += 1
                ins.then_inc(sem("act_step"), 1)
                act.wait_ge(sem("act_step"), own[0])

            def step(n):
                ahead(split_hi, act, n)

            def turn(name):
                for u in range(4):
                    b, half = u // 2, u % 2
                    g = 4 * TURNS[name] + u
                    act.wait_ge(sem("turn_scaled"), g + 1)
                    act.activation(sthi[:, b, 4 * half:4 * half + 4, :].rearrange("p k t -> p (k t)"), scaled[:, g % 2, :],
                                   ACT.Copy).then_inc(sem("turn_hi"), 1)

            def squares(name, dst, src):
                if SQ[name]:
                    act.wait_ge(sem("sq_summed"), SQ[name])
                act.activation(dst, src, ACT.Square).then_inc(sem("sq_done"), 1)

            act.wait_ge(sem("params"), 16)
            act.activation(rthi[:, :, :].rearrange("p k e -> p (k e)"), prm[:, ROUT:ROUT + KT * E_], ACT.Copy)\
                .then_inc(sem("router_hi"), 1)
            for n in range(SPLIT):
                split_hi(act, n, shape_of(n))
            for l in range(DEPTH):
                turn(f"mem{l}")
                for h in range(2):
                    step(KV0 + 2 * l + h)
                act.activation(mval[:, l, :, :], ps[:, 2 * l:2 * l + 2, QK:2 * QK], ACT.Copy).then_inc(sem("mv_copied"), 1)
                squares(f"mk{l}", sq_early[:, :, 0:QK], ps[:, 2 * l:2 * l + 2, 0:QK])

            def mixer(l, n):
                v = l + 1
                turn(f"att{l}")
                step(n)
                step(n + 1)
                squares(f"fqk{l}", sq_early[:, :, :], ps[:, 0:2, :])
                step(n + 2)
                act.wait_ge(sem("z_ready"), v)
                then(act.activation(st[:, 88:96], st[:, 80:88], ACT.Exp, scale=-1.0))
                act.activation(st[:, 96:104], st[:, 88:96], ACT.Ln, bias=1.0).then_inc(sem("ln_done"), 1)
                step(n + 3)
                squares(f"mq{l}", sq_early[:, :, 0:QK], ps[:, 0:2, 0:QK])
                step(n + 4)
                step(n + 5)
                act.wait_ge(sem("f_turned"), v)
                act.activation(fT[0:66, H:2 * H, :].rearrange("p h t -> p (h t)"),
                               ps[0:66, 6:8, :].rearrange("p c t -> p (c t)"), ACT.Copy,
                               scale=prm[0:66, G_FK + l:G_FK + l + 1]).then_inc(sem("f_T"), 1)
                step(n + 6)
                step(n + 7)
                act.activation(rval[:, :, :], ps[:, 0:2, :], ACT.Copy).then_inc(sem("rv_copied"), 1)

                def exps(b, src, dst, at, maxed, done):
                    act.wait_ge(sem(maxed), NB * l + b + 1)
                    for a in range(H):
                        c = at + b * H + a
                        last = act.activation(dst[:, a, :], src(a), ACT.Exp, bias=st[:, c:c + 1],
                                              accum_out=st[:, c + 8:c + 9])
                    last.then_inc(sem(done), 1)

                exps(0, lambda a: ps[:, 4, a * P:(a + 1) * P], pf0, 32, "f_max", "f_exp")
                exps(1, lambda a: ps[:, 5 + a // 2, (a % 2) * SEQ:(a % 2 + 1) * SEQ], pf1, 32, "f_max", "f_exp")
                act.wait_ge(sem("r_turned"), v)
                act.activation(rT.rearrange("p c t -> p (c t)"), ps[:, 2:4, :].rearrange("p c t -> p (c t)"), ACT.Copy)\
                    .then_inc(sem("r_T"), 1)
                step(n + 8)
                step(n + 9)
                act.activation(yret, ps[:, 0:2, :], ACT.Silu).then_inc(sem("gate_silu"), 1)
                act.wait_ge(sem("f_pturned"), NB * l + 1)
                act.activation(fpT0.rearrange("p h t -> p (h t)"), ps[:, 4, :], ACT.Copy).then_inc(sem("f_pT"), 1)
                exps(0, lambda a: ps[:, 2 + a // 2, (a % 2) * SEQ:(a % 2 + 1) * SEQ], pm[0], 48, "m_max", "m_exp")
                act.wait_ge(sem("f_out"), v)
                squares(f"fo{l}", scaled[:, :, 0:QK], yfox)
                exps(1, lambda a: ps[:, 4 + a // 2, (a % 2) * SEQ:(a % 2 + 1) * SEQ], pm[1], 48, "m_max", "m_exp")
                act.wait_ge(sem("m_pturned"), NB * l + 1)
                act.activation(mpT[0].rearrange("p h t -> p (h t)"), ps[:, 2:4, :].rearrange("p c t -> p (c t)"), ACT.Copy)\
                    .then_inc(sem("m_pT"), 1)
                act.wait_ge(sem("r_valued"), v)
                squares(f"ro{l}", scaled[:, :, :], ps[:, 0:2, :])
                act.wait_ge(sem("m_out"), v)
                squares(f"mo{l}", scaled[:, :, 0:QK], ymem)
                turn(f"out{l}")
                for q in range(4):
                    step(n + 10 + q)

            def silus(it, c, nb, bank, unit):
                for b in range(nb):
                    if unit + b >= nb:
                        act.wait_ge(sem("hidden_ready"), counted(unit + b - nb + 1, it, 2 * NCH))
                    act.activation(sil[:, b, 0:CH[c]], ps[:, bank + b, 0:CH[c]], ACT.Silu).then_inc(sem("silu_done"), 1)

            def hidden_hi(it, c, nb, bank, unit):
                for b in range(nb):
                    act.wait_ge(sem("hid_turned"), counted(unit + b + 1, it, 2 * NCH))
                    full, rest = CH[c] // P, CH[c] % P
                    last = act.activation(hidhi[:, b, 0:full, :].rearrange("p k t -> p (k t)"), ps[:, bank + b, 0:full * P],
                                          ACT.Copy)
                    if rest:
                        last = act.activation(hidhi[0:rest, b, full, :], ps[0:rest, bank + b, full * P:(full + 1) * P], ACT.Copy)
                    last.then_inc(sem("hid_hi"), 1)

            mixer(0, IN0)
            turn("ffn0")
            n = DENSE0
            for c in range(NCH):
                step(n)
                if c:
                    hidden_hi(0, c - 1, NB, 2, NB * (c - 1))
                step(n + 1)
                silus(0, c, NB, 0, NB * c)
                for i in range(4 if c else 2):
                    step(n + 2 + i)
                n += LPC if c else 4
            hidden_hi(0, NCH - 1, NB, 2, NB * (NCH - 1))
            step(n)
            step(n + 1)
            mixer(1, IN1)
            turn("ffn1")
            act.wait_ge(sem("rows_ready"), NB * (ROWS["ffn1"] + 1))
            act.activation(tokhi[:, :, :], tok[:, :, :], ACT.Copy).then_inc(sem("rows_hi"), 1)
            act.wait_ge(sem("top_two"), 1)
            act.activation(st[:, 108:110], st[:, 106:108], ACT.Exp).then_inc(sem("gate_exp"), 1)

            def onehot_out(k, it, par):
                act.wait_ge(sem("onehot_turned"), counted(k + 1, it, 2))
                act.activation(onehotT[:, par, :, :].rearrange("p b t -> p (b t)"), ps[:, 3, 0:NB * P], ACT.Copy)\
                    .then_inc(sem("onehot_T"), 1)

            def gathered_hi(k, it, par, half):
                act.wait_ge(sem("gathered_scaled"), counted(2 * k + half + 1, it, 4))
                act.activation(sthi[:, par, 4 * half:4 * half + 4, :].rearrange("p k t -> p (k t)"), scaled[:, half, :],
                               ACT.Copy).then_inc(sem("gathered_hi"), 1)

            def out_copy(k, it):
                if k or not isinstance(it, int):
                    act.wait_ge(sem("scattered"), counted(2 * k, it, 4))
                act.activation(outhi[:, :], ps[:, 4:6, :].rearrange("p c n -> p (c n)"), ACT.Copy).then_inc(sem("out_hi"), 1)

            def expert_pair(rnd, it):
                def after(par, c, what, n):
                    k = rnd * E_ + par
                    u = DENSE_UNITS + k * NCH + c
                    before = not (isinstance(it, int) and par == 0)
                    if what in (("gate", 1), ("down", 1)) and (what[0] == "gate" or c == 0):
                        used(act, n, it)
                    if what == ("gate", 1):
                        silus(it, c, 1, 0, u)
                        if c or before:
                            hidden_hi(it, (c - 1) % NCH, 1, 1, u - 1)
                    if what == ("down", 0) and c == 2:
                        onehot_out(k + 1, it, 1 - par)
                    if what == ("down", 1) and c in (3, 4):
                        gathered_hi(k + 1, it, 1 - par, c - 3)
                    if what == ("down", 1) and c == 0:
                        out_copy(k - 1, it)
                split_pair(split_hi, act, rnd, it, after)

            def expert_round(rnd):
                expert_pair(rnd, 0)
                with act.Fori(1, E_ // 2) as it:
                    expert_pair(rnd, it)
                n0 = MOE0 + (rnd + 1) * MOE_LOADS - 2
                for h in range(2):
                    split_hi(act, n0 + h, FLUSH[h])
                hidden_hi(0, NCH - 1, 1, 1, DENSE_UNITS + (rnd + 1) * E_ * NCH - 1)
                used(act, n0 + 1)
                out_copy((rnd + 1) * E_ - 1, 0)

            onehot_out(0, 0, 0)
            for half in range(2):
                gathered_hi(0, 0, 0, half)
            expert_round(0)
            act.wait_ge(sem("flag_ready"), 1)
            with act.If(act.value_load(flag[0:1, 0:1], min_val=0, max_val=1) > 0):
                expert_round(1)
            with act.Else():
                act.nop()

        @block.vector
        def _(dve):
            own = [0]

            def then(ins):
                own[0] += 1
                ins.then_inc(sem("dve_step"), 1)
                dve.wait_ge(sem("dve_step"), own[0])

            def step(n):
                ahead(split_lo, dve, n)

            def flat(t):
                return t.rearrange("p k t -> p (k t)")

            def scale_unit(src, gain, half, dst, done):
                g = prm[:, gain + 4 * half:gain + 4 * half + 4].unsqueeze(2).to_broadcast([P, 4, P])
                dve.tensor_tensor(dst.rearrange("p (k t) -> p k t", k=4), src.rearrange("p (k t) -> p k t", k=4),
                                  g, ALU.mult).then_inc(sem(done), 1)

            def turn(name):
                def lo(u):
                    g = 4 * TURNS[name] + u
                    b, half = u // 2, u % 2
                    dve.wait_ge(sem("turn_hi"), g + 1)
                    dve.tensor_tensor(flat(stlo[:, b, 4 * half:4 * half + 4, :]), scaled[:, g % 2, :],
                                      flat(sthi[:, b, 4 * half:4 * half + 4, :]).bitcast(F32), ALU.subtract)\
                        .then_inc(sem("turn_lo"), 1)
                for u in range(4):
                    g = 4 * TURNS[name] + u
                    dve.wait_ge(sem("turned"), g + 1)
                    if g >= 2:
                        dve.wait_ge(sem("turn_lo"), g - 1)
                    scale_unit(ps[:, 4 + g % 2, :], GAIN[name], u % 2, scaled[:, g % 2, :], "turn_scaled")
                    if u:
                        lo(u - 1)
                lo(3)

            def inverse_rms(n, width):
                x, y, t, h = st[:, 0:n], st[:, 16:16 + n], guess[:, 0:n], newton[:, 0:n]
                then(dve.tensor_scalar(x, x, 1.0 / width, EPS, ALU.mult, ALU.add))
                then(dve.tensor_scalar(t, x.bitcast(I32), 1, None, ALU.logical_shift_right))
                then(dve.tensor_scalar(y.bitcast(I32), t, -1.0, float(0x5F3759DF), ALU.mult, ALU.add))
                then(dve.tensor_scalar(x, x, -0.5, None, ALU.mult))
                for _ in range(3):
                    then(dve.tensor_tensor(h, y, y, ALU.mult))
                    then(dve.tensor_tensor(h, h, x, ALU.mult))
                    then(dve.scalar_tensor_tensor(out=y, in0=h, scalar=1.5, in1=y, op0=ALU.add, op1=ALU.mult))

            def norm_rows(src):
                for b in range(NB):
                    then(dve.tensor_tensor_reduce(out=scaled[:, :, :].rearrange("p a n -> p (a n)"), in0=src[:, b, :],
                                                  in1=src[:, b, :], scale=1.0, scalar=0.0, op0=ALU.mult, op1=ALU.add,
                                                  accum_out=st[:, b:b + 1]))
                inverse_rms(NB, D)
                for b in range(NB):
                    dve.tensor_scalar(tok[:, b, :], src[:, b, :], st[:, 16 + b:17 + b], None, ALU.mult)\
                        .then_inc(sem("rows_ready"), 1)

            def head_scales(name, sq, width, hh):
                dve.wait_ge(sem("sq_done"), SQ[name] + 1)
                dve.tensor_reduce(st[:, 0:NB * hh].rearrange("p (b h) -> p b h", b=NB),
                                  sq.rearrange("p b (h d) -> p b h d", d=width), AX.X, ALU.add)\
                    .then_inc(sem("sq_summed"), 1)
                dve.wait_ge(sem("sq_summed"), SQ[name] + 1)
                inverse_rms(NB * hh, width)
                return st[:, 16:16 + NB * hh].rearrange("p (b h) -> p b h", b=NB)

            def by_head(dst, src, scales, width):
                hh = scales.shape[2]
                return dve.tensor_tensor(dst if len(dst.shape) == 4 else dst.rearrange("p b (h d) -> p b h d", d=width),
                                         src.rearrange("p b (h d) -> p b h d", d=width),
                                         scales.unsqueeze(3).to_broadcast([P, NB, hh, width]), ALU.mult)

            dve.wait_ge(sem("tables"), 16)
            dve.tensor_copy(idb[:, :], ident).then_inc(sem("mask_ready"), 1)
            dve.tensor_copy(maskb[:, :], tb[:, T_MASK:T_MASK + P]).then_inc(sem("mask_ready"), 1)
            dve.wait_ge(sem("mem_in"), 16)
            norm_rows(tok)
            dve.wait_ge(sem("router_hi"), 1)
            dve.tensor_tensor(flat(rtlo[:, :, :]), prm[:, ROUT:ROUT + KT * E_], flat(rthi[:, :, :]).bitcast(F32),
                              ALU.subtract).then_inc(sem("router_lo"), 1)
            for n in range(SPLIT):
                split_lo(dve, n, shape_of(n))

            def memory_keys(l):
                r = head_scales(f"mk{l}", sq_early[:, :, 0:QK], DH, H)
                if l:
                    dve.wait_ge(sem("mk_turned"), l)
                by_head(rqk[:, :, 0:QK], ps[:, 2 * l:2 * l + 2, 0:QK], r, DH).then_inc(sem("mk_rows"), 1)
                dve.wait_ge(sem("mk_turned"), l + 1)
                dve.tensor_scalar(flat(mkT[:, l, :, :]), ps[:, 6, :], prm[:, G_MK + l:G_MK + l + 1], None, ALU.mult)\
                    .then_inc(sem("mk_T"), 1)

            for l in range(DEPTH):
                turn(f"mem{l}")
                for h in range(2):
                    step(KV0 + 2 * l + h)
                memory_keys(l)

            def mixer(l, n):
                v = l + 1
                if l == 0:
                    dve.wait_ge(sem("x_in"), 16)
                norm_rows(xres)
                turn(f"att{l}")
                dve.memset(aug[:, :, 0:H, DH + 1:DH + 2], 1.0)
                dve.memset(aug[:, :, H:2 * H, DH:DH + 1], 1.0)
                step(n)
                step(n + 1)
                r = head_scales(f"fqk{l}", sq_early[:, :, :], DH, 2 * H)
                then(dve.tensor_scalar(r[:, :, 0:H], r[:, :, 0:H], SCALE, None, ALU.mult))
                by_head(aug[:, :, :, 0:DH], ps[:, 0:2, :], r, DH).then_inc(sem("fqk_rows"), 1)
                step(n + 2)
                z, az = (st[:, a:a + 8] for a in (72, 80))
                pair = lambda t: t.rearrange("p (b h) -> p b h", b=NB)
                used(dve, n + 2)
                then(dve.tensor_tensor(pair(z), ps[:, 2:4, QK:QK + H],
                                       prm[:, BIAS + H * l:BIAS + H * (l + 1)].unsqueeze(1).to_broadcast([P, NB, H]), ALU.add))
                dve.scalar_tensor_tensor(out=az, in0=z, scalar=-1.0, in1=z, op0=ALU.mult, op1=ALU.max).then_inc(sem("z_ready"), 1)
                dve.tensor_copy(fval, ps[:, 2:4, 0:QK]).then_inc(sem("fv_copied"), 1)
                dve.wait_ge(sem("ln_done"), v)
                dve.scalar_tensor_tensor(out=st[:, 64:72], in0=z, scalar=0.0, in1=st[:, 96:104], op0=ALU.min,
                                         op1=ALU.subtract).then_inc(sem("logf"), 1)
                step(n + 3)
                r = head_scales(f"mq{l}", sq_early[:, :, 0:QK], DH, H)
                by_head(ymem, ps[:, 0:2, 0:QK], r, DH).then_inc(sem("mq_rows"), 1)
                dve.wait_ge(sem("logf_summed"), v)
                sums = ps[:, 6, 0:8].rearrange("p (b h) -> p b h", b=NB).unsqueeze(3)
                dve.tensor_copy(aug[:, :, 0:H, DH:DH + 1], sums)
                dve.tensor_scalar(aug[:, :, H:2 * H, DH + 1:DH + 2], sums, -1.0, None, ALU.mult).then_inc(sem("aug_ready"), 1)
                step(n + 4)
                step(n + 5)
                dve.wait_ge(sem("f_turned"), v)
                dve.tensor_scalar(flat(fT[0:66, 0:H, :]), flat(ps[0:66, 4:6, :]), prm[0:66, G_FQ + l:G_FQ + l + 1], None,
                                  ALU.mult).then_inc(sem("f_T"), 1)
                src = ps[:, 2:4, :].rearrange("p b (h c i) -> p b h c i", c=2, i=32)
                dst = rqk.rearrange("p b (h c i) -> p b h c i", c=2, i=32)
                cs, sn = (t.unsqueeze(2).to_broadcast([P, NB, 8, 32]) for t in (cos, sin))
                for c, op in ((0, ALU.subtract), (1, ALU.add)):
                    tmp = sq_early[:, :, c * QK:(c + 1) * QK].rearrange("p b (h i) -> p b h i", i=32)
                    dve.tensor_tensor(dst[:, :, :, c, :], src[:, :, :, c, :], cs, ALU.mult)
                    then(dve.tensor_tensor(tmp, src[:, :, :, 1 - c, :], sn, ALU.mult))
                    last = dve.tensor_tensor(dst[:, :, :, c, :], dst[:, :, :, c, :], tmp, op)
                last.then_inc(sem("r_rotated"), 1)
                step(n + 6)
                step(n + 7)

                def maxima(b, src, at, scored, done):
                    dve.wait_ge(sem(scored), NB * l + b + 1)
                    c = at + b * H
                    dve.tensor_reduce(st[:, c:c + H], src, AX.X, ALU.max, negate=True).then_inc(sem(done), 1)

                maxima(0, ps[:, 4, :].rearrange("p (h k) -> p h k", h=H), 32, "f_scored", "f_max")
                maxima(1, ps[:, 5:7, :].rearrange("p c (h k) -> p (c h) k", h=2), 32, "f_scored", "f_max")
                dve.wait_ge(sem("mq_turned"), v)
                dve.tensor_scalar(flat(mqT), ps[:, 7, :], prm[:, G_MQ + l:G_MQ + l + 1], SCALE, ALU.mult, ALU.mult)\
                    .then_inc(sem("mq_T"), 1)
                step(n + 8)
                step(n + 9)
                dve.wait_ge(sem("f_pturned"), NB * l + 2)
                dve.tensor_copy(flat(fpT1), flat(ps[:, 5:7, :])).then_inc(sem("f_pT"), 1)
                maxima(0, ps[:, 2:4, :].rearrange("p c (h k) -> p (c h) k", h=2), 48, "m_scored", "m_max")

                def weigh(dst, bank, at):
                    s, r = (st[:, a:a + 8].rearrange("p (b h) -> p b h", b=NB) for a in (at + 8, 112))
                    then(dve.reciprocal(r, s))
                    return by_head(dst, ps[:, bank, :].rearrange("p (b d) -> p b d", b=NB), r, DH)

                dve.wait_ge(sem("f_valued"), v)
                weigh(yfox, 7, 32 + 0).then_inc(sem("f_out"), 1)
                maxima(1, ps[:, 4:6, :].rearrange("p c (h k) -> p (c h) k", h=2), 48, "m_scored", "m_max")
                dve.wait_ge(sem("r_scored"), 2 * l + 1)
                dve.tensor_tensor(flat(rpT0), flat(ps[:, 0:2, :]), flat(decay), ALU.mult).then_inc(sem("r_decayed"), 1)
                dve.wait_ge(sem("r_scored"), 2 * l + 2)
                dve.tensor_tensor(rpT1.rearrange("p (c h) i -> p c h i", c=2),
                                  ps[:, 6:8, 0:2 * P].rearrange("p c (h i) -> p c h i", h=2),
                                  decay[:, :, 0:P].rearrange("p (c h) i -> p c h i", c=2), ALU.mult).then_inc(sem("r_decayed"), 1)
                r = head_scales(f"fo{l}", scaled[:, :, 0:QK], DH, H)
                by_head(yfox, yfox, r, DH)
                dve.wait_ge(sem("m_pturned"), NB * l + 2)
                dve.tensor_copy(flat(mpT[1]), flat(ps[:, 4:6, :])).then_inc(sem("m_pT"), 1)
                r = head_scales(f"ro{l}", scaled[:, :, :], RDV, RH)
                then(by_head(sq_early[:, :, :], ps[:, 0:2, :], r, RDV))
                dve.tensor_tensor(yret, yret, sq_early[:, :, :], ALU.mult)
                dve.wait_ge(sem("m_valued"), v)
                ins = weigh_mem(ps[:, 6, :])
                ins.then_inc(sem("m_out"), 1)
                r = head_scales(f"mo{l}", scaled[:, :, 0:QK], DH, H)
                for b in range(NB):
                    dve.tensor_tensor(ymem[:, b, :].rearrange("p (h d) -> p h d", d=DH),
                                      ymem[:, b, :].rearrange("p (h d) -> p h d", d=DH),
                                      r[:, b, :].unsqueeze(2).to_broadcast([P, H, DH]), ALU.mult)\
                        .then_inc(sem("rows_ready"), 1)
                turn(f"out{l}")
                for q in range(4):
                    step(n + 10 + q)
                used(dve, n + 13)
                for b in range(NB):
                    dve.tensor_tensor(xres[:, b, :], xres[:, b, :], flat(ps[:, 2 * b:2 * b + 2, :]), ALU.add)\
                        .then_inc(sem("x_added"), 1)

            def weigh_mem(src):
                s = st[:, 56:64].rearrange("p (b c h) -> p b h c", b=NB, c=2)
                r = st[:, 112:120].rearrange("p (b h c) -> p b h c", b=NB, c=2)
                then(dve.reciprocal(r, s))
                return by_head(ymem, src.rearrange("p (b d) -> p b d", b=NB),
                               st[:, 112:120].rearrange("p (b h) -> p b h", b=NB), DH)

            def hidden(it, c, nb, bank, unit):
                for b in range(nb):
                    dve.wait_ge(sem("silu_done"), counted(unit + b + 1, it, 2 * NCH))
                    if unit + b >= nb:
                        dve.wait_ge(sem("hid_turned"), counted(unit + b - nb + 1, it, 2 * NCH))
                    dve.tensor_tensor(hid[:, b, 0:CH[c]], sil[:, b, 0:CH[c]], ps[:, bank + b, 0:CH[c]], ALU.mult)\
                        .then_inc(sem("hidden_ready"), 1)

            def hidden_lo(it, c, nb, bank, unit):
                for b in range(nb):
                    dve.wait_ge(sem("hid_hi"), counted(unit + b + 1, it, 2 * NCH))
                    full, rest = CH[c] // P, CH[c] % P
                    last = dve.tensor_tensor(flat(hidlo[:, b, 0:full, :]), ps[:, bank + b, 0:full * P],
                                             flat(hidhi[:, b, 0:full, :]).bitcast(F32), ALU.subtract)
                    if rest:
                        last = dve.tensor_tensor(hidlo[0:rest, b, full, :], ps[0:rest, bank + b, full * P:(full + 1) * P],
                                                 hidhi[0:rest, b, full, :].bitcast(F32), ALU.subtract)
                    last.then_inc(sem("hid_lo"), 1)

            mixer(0, IN0)
            dve.wait_ge(sem("x_added"), NB)
            norm_rows(xres)
            turn("ffn0")
            n = DENSE0
            for c in range(NCH):
                step(n)
                if c:
                    hidden_lo(0, c - 1, NB, 2, NB * (c - 1))
                step(n + 1)
                for i in range(4 if c else 2):
                    step(n + 2 + i)
                n += LPC if c else 4
                used(dve, n - 1)
                hidden(0, c, NB, 2, NB * c)
            hidden_lo(0, NCH - 1, NB, 2, NB * (NCH - 1))
            step(n)
            step(n + 1)
            used(dve, n + 1)
            for b in range(NB):
                dve.tensor_tensor(xres[:, b, :], xres[:, b, :], flat(ps[:, 4 + 2 * b:6 + 2 * b, :]), ALU.add)\
                    .then_inc(sem("x_added"), 1)
            dve.wait_ge(sem("x_added"), 2 * NB)
            mixer(1, IN1)
            dve.wait_ge(sem("x_added"), 3 * NB)
            norm_rows(xres)
            turn("ffn1")
            dve.wait_ge(sem("rows_hi"), 1)
            dve.tensor_tensor(toklo[:, :, :], tok[:, :, :], tokhi[:, :, :].bitcast(F32), ALU.subtract).then_inc(sem("rows_split"), 1)

            dve.wait_ge(sem("logits"), 1)
            lg = st[:, 0:NB * E_].rearrange("p (b e) -> p b e", b=NB)
            then(dve.tensor_copy(lg, ps[:, 6, 0:NB * E_].rearrange("p (b e) -> p b e", b=NB)))
            for b in range(NB):
                then(dve.max(mx[:, b, :], lg[:, b, :]))
                then(dve.max_index(mi[:, b, :], mx[:, b, :], lg[:, b, :]))
            then(dve.tensor_copy(mif[:, :, :], mi[:, :, :]))
            dve.tensor_tensor(st[:, 106:108].unsqueeze(2), mx[:, :, 1:2], mx[:, :, 0:1], ALU.subtract)\
                .then_inc(sem("top_two"), 1)
            iota = tb[:, T_IOTA:T_IOTA + P]
            for b in range(NB):
                then(dve.tensor_scalar(sel[:, b, :], iota[:, 0:E_], mif[:, b, 0:1], None, ALU.is_equal))
                then(dve.scalar_tensor_tensor(out=sel[:, b, :], in0=iota[:, 0:E_], scalar=mif[:, b, 1:2], in1=sel[:, b, :],
                                              op0=ALU.is_equal, op1=ALU.add))
            dve.memset(slot_of[:, :, :], -1.0).then_inc(sem("chosen"), 1)
            dve.wait_ge(sem("gate_exp"), 1)
            g0, g1, den = st[:, 120:122], st[:, 122:124], st[:, 124:126]
            then(dve.tensor_scalar(den, st[:, 108:110], 1.0, None, ALU.add))
            then(dve.reciprocal(g0, den))
            then(dve.tensor_tensor(g1, g0, st[:, 108:110], ALU.mult))
            for b in range(NB):
                then(dve.tensor_scalar(comb[:, b, :], iota[:, 0:E_], mif[:, b, 0:1], g0[:, b:b + 1], ALU.is_equal, ALU.mult))
                then(dve.tensor_scalar(st[:, 40:48], iota[:, 0:E_], mif[:, b, 1:2], g1[:, b:b + 1], ALU.is_equal, ALU.mult))
                then(dve.tensor_tensor(comb[:, b, :], comb[:, b, :], st[:, 40:48], ALU.add))
            dve.wait_ge(sem("ranked"), 1)
            upto = ps[:, 7, 0:NB * E_].rearrange("p (b e) -> p b e", b=NB)
            then(dve.tensor_tensor(slot_of[:, :, 0:E_], upto, sel[:, :, :], ALU.mult))
            then(dve.tensor_scalar(slot_of[:, :, 0:E_], slot_of[:, :, 0:E_], -1.0, None, ALU.add))
            then(dve.tensor_scalar(slot_of[:, :, E_:2 * E_], slot_of[:, :, 0:E_], float(-P), None, ALU.add))
            then(dve.tensor_reduce(st[:, 126:127], ps[:, 7, NB * E_:(NB + 1) * E_], AX.X, ALU.max))
            then(dve.tensor_scalar(flag[:, :], st[:, 126:127], float(P), None, ALU.is_gt))
            dve.memset(st[:, 127:128], 0.0).then_inc(sem("flag_ready"), 1)

            def onehot_in(k, it):
                if k:
                    dve.wait_ge(sem("gathered"), counted(2 * k, it, 4))
                for b in range(NB):
                    col = slot_of[:, b, k:k + 1] if isinstance(it, int) else slot_of[:, b, bass.ds(it * 2 + k, 1)]
                    last = dve.tensor_scalar(onehot[:, b, :], iota, col, None, ALU.is_equal)
                last.then_inc(sem("onehot_ready"), 1)

            def gathered_scale(k, it, half):
                dve.wait_ge(sem("gathered"), counted(2 * k + half + 1, it, 4))
                if k:
                    dve.wait_ge(sem("gathered_lo"), counted(2 * k + half - 1, it, 4))
                else:
                    dve.wait_ge(sem("turn_lo"), 4 * len(TURNS))
                scale_unit(ps[:, 3, :], GAIN["ffn1"], half, scaled[:, half, :], "gathered_scaled")

            def gathered_rest(k, it, par, half):
                dve.wait_ge(sem("gathered_hi"), counted(2 * k + half + 1, it, 4))
                dve.tensor_tensor(flat(stlo[:, par, 4 * half:4 * half + 4, :]), scaled[:, half, :],
                                  flat(sthi[:, par, 4 * half:4 * half + 4, :]).bitcast(F32), ALU.subtract)\
                    .then_inc(sem("gathered_lo"), 1)

            def out_rest(k, it):
                dve.wait_ge(sem("out_hi"), counted(k + 1, it, 2))
                dve.tensor_tensor(outlo[:, :], flat(ps[:, 4:6, :]), outhi[:, :].bitcast(F32), ALU.subtract).then_inc(sem("out_copied"), 1)

            def scatter_add(k, e, it, b):
                dve.wait_ge(sem("scattered"), counted(2 * k + b + 1, it, 4))
                gate = comb[:, b, e:e + 1] if isinstance(it, int) else comb[:, b, bass.ds(it * 2 + e, 1)]
                if k or b or not isinstance(it, int):
                    dve.wait_ge(sem("scatter_added"), counted(2 * k + b, it, 4))
                dve.scalar_tensor_tensor(out=xres[:, b, :], in0=flat(ps[:, 6:8, :]), scalar=gate, in1=xres[:, b, :],
                                         op0=ALU.mult, op1=ALU.add).then_inc(sem("scatter_added"), 1)

            def expert_pair(rnd, it):
                def after(par, c, what, n):
                    k = rnd * E_ + par
                    u = DENSE_UNITS + k * NCH + c
                    before = not (isinstance(it, int) and par == 0)
                    if what in (("gate", 1), ("up", 1)):
                        used(dve, n, it)
                    if what == ("gate", 1) and (c or before):
                        hidden_lo(it, (c - 1) % NCH, 1, 1, u - 1)
                    if what == ("up", 1):
                        hidden(it, c, 1, 2, u)
                    if what == ("gate", 1) and c == 2:
                        onehot_in(k + 1, it)
                    if what == ("down", 0) and c in (3, 4):
                        gathered_scale(k + 1, it, c - 3)
                    if what == ("down", 1) and c in (3, 4):
                        gathered_rest(k + 1, it, 1 - par, c - 3)
                    if what == ("down", 1) and c == 0:
                        out_rest(k - 1, it)
                    if what == ("down", 1) and c in (1, 2) and before:
                        scatter_add(k - 1, par - 1, it, c - 1)
                split_pair(split_lo, dve, rnd, it, after)

            def expert_round(rnd):
                expert_pair(rnd, 0)
                with dve.Fori(1, E_ // 2) as it:
                    expert_pair(rnd, it)
                n0 = MOE0 + (rnd + 1) * MOE_LOADS - 2
                for h in range(2):
                    split_lo(dve, n0 + h, FLUSH[h])
                hidden_lo(0, NCH - 1, 1, 1, DENSE_UNITS + (rnd + 1) * E_ * NCH - 1)
                k = (rnd + 1) * E_ - 1
                out_rest(k, 0)
                for b in range(NB):
                    scatter_add(k, E_ - 1, 0, b)
                dve.wait_ge(sem("scatter_added"), 2 * (k + 1))

            onehot_in(0, 0)
            for half in range(2):
                gathered_scale(0, 0, half)
                gathered_rest(0, 0, 0, half)
            expert_round(0)
            dve.wait_ge(sem("flag_ready"), 1)
            with dve.If(dve.value_load(flag[0:1, 0:1], min_val=0, max_val=1) > 0):
                expert_round(1)
            with dve.Else():
                dve.nop()
            dve.memset(st[:, 0:1], 0.0).then_inc(sem("x_final"), 1)


def tables():
    t = np.zeros((P, NTAB), np.float32)
    heads = np.arange(RH, dtype=np.float32)
    log_g = np.log1p(-np.exp2(-5.0 - heads)).astype(np.float64)
    j, i = np.arange(P)[:, None], np.arange(SEQ)[None, :]
    dec = t[:, T_DEC:T_DEC + 4 * SEQ].reshape(P, RH, SEQ)
    for h in range(RH):
        dec[:, HEAD_AT[h], :] = np.where(i >= j, np.exp(log_g[h] * np.maximum(i - j, 0)), 0.0) * SCALE
    t[:, T_DEC:T_DEC + 4 * SEQ] = dec.reshape(P, -1)
    pos = (np.arange(NB)[None, :, None] * P + np.arange(P)[:, None, None]).astype(np.float32)
    freq = (np.float32(10000.0) ** (-np.arange(32, dtype=np.float32) / np.float32(32))).astype(np.float32)
    ang = (pos * freq[None, None, :]).astype(np.float32).astype(np.float64)
    t[:, T_COS:T_COS + NB * 32] = np.cos(ang).reshape(P, -1)
    t[:, T_SIN:T_SIN + NB * 32] = np.sin(ang).reshape(P, -1)
    t[:, T_ID:T_ID + P] = np.eye(P)
    r, c = np.arange(P)[:, None], np.arange(P)[None, :]
    t[:, T_TRI:T_TRI + P] = r <= c
    t[:, T_ONE:T_ONE + P] = 1.0
    t[:, T_MASK:T_MASK + P] = np.where(c <= r, 0.0, NEG)
    t[:, T_IOTA:T_IOTA + P] = c
    return t


def parameters(a):
    p = np.zeros((P, NPAR), np.float32)
    for name, at in (("attn_norm_g", G_ATT), ("ffn_norm_g", G_FFN), ("out_norm_g", G_OUT), ("mem_norm_g", G_MEM)):
        for l in range(DEPTH):
            p[:, at + KT * l:at + KT * (l + 1)] = a[name][l].reshape(KT, P).T
    for name, at in (("fox_q_norm_g", G_FQ), ("fox_k_norm_g", G_FK)):
        for l in range(DEPTH):
            p[0:DH, at + l] = a[name][l]
            p[DH:DH + 2, at + l] = 1.0
    for name, at in (("mem_q_norm_g", G_MQ), ("mem_k_norm_g", G_MK)):
        for l in range(DEPTH):
            p[0:DH, at + l] = a[name][l]
            p[DH:2 * DH, at + l] = a[name][l]
    for l in range(DEPTH):
        p[:, BIAS + H * l:BIAS + H * (l + 1)] = a["forget_bias"][l][None, :]
    p[:, ROUT:ROUT + KT * E_] = a["router_w"][0].reshape(KT, P, E_).transpose(1, 0, 2).reshape(P, KT * E_)
    return p


_INS = ["x", "mem", "w_in", "w_mem_kv", "w_out", "dense_w_gate", "dense_w_up", "dense_w_down",
        "expert_w_gate", "expert_w_up", "expert_w_down"]


def kernel(**inputs):
    import concourse.bacc as bacc
    from concourse.bass_utils import run_bass_kernel_spmd

    nc = bacc.Bacc("TRN2", target_bir_lowering=False, num_devices=1, dynamic_dma_scratch_size=1024)
    host = {k: np.ascontiguousarray(np.asarray(v)) for k, v in inputs.items()}
    arrays = {f"in_{n}": host[n] for n in _INS}
    arrays["in_par"] = parameters(host)
    arrays["in_tab"] = tables()
    args = [nc.dram_tensor(n, a.shape, F32, kind="ExternalInput").ap() for n, a in arrays.items()]
    args.append(nc.dram_tensor("out_x", (1, SEQ, D), F32, kind="ExternalOutput").ap())
    build(nc, *args)
    r = run_bass_kernel_spmd(nc, [arrays], core_ids=[0])
    return r.results[0]["out_x"]
```

```python
from contextlib import ExitStack

import numpy as np
import concourse.bass as bass
from concourse import mybir

F32 = mybir.dt.float32
F32R = mybir.dt.float32r
BF16 = mybir.dt.bfloat16
I32 = mybir.dt.int32
U32 = mybir.dt.uint32
ACT = mybir.ActivationFunctionType
ALU = mybir.AluOpType
AX = mybir.AxisListType

P = 128
SEQ, D = 256, 1024
NB = SEQ // P
KT = D // P
DEPTH = 2
RH, RDV = 4, 128
DH = 64
H = 4
QK = H * DH
EPS = 1e-6
SCALE = DH ** -0.5
D_FF = 2752
E_ = 8
W = 512
LAST = D_FF - (D_FF // W - 1) * W
CH = [W] * (D_FF // W - 1) + [-(-LAST // 256) * 128, LAST - -(-LAST // 256) * 128]
C0 = [sum(CH[:c]) for c in range(len(CH))]
assert all(256 < n <= W for n in CH)
NCH = len(CH)
RAW, SPLIT = 9, 3
SLOT = 2080
LPC = 6
assert (LPC * NCH) % RAW == 0 and RAW % SPLIT == 0
NEG = -1e30

RQ, RV, RG, FQ, FV, FF, MQ = 0, 512, 1024, 1536, 2048, 2304, 2308

G_ATT, G_FFN, G_OUT, G_MEM = 0, 16, 32, 48
G_FQ, G_FK, G_MQ, G_MK = 64, 66, 68, 70
BIAS, ROUT = 72, 80
NPAR = ROUT + KT * E_
T_ID = 0
T_DEC = T_ID + P
T_COS = T_DEC + 4 * SEQ
T_SIN = T_COS + NB * 32
T_TRI = T_SIN + NB * 32
T_ONE = T_TRI + P
T_MASK = T_ONE + P
T_IOTA = T_MASK + P
NTAB = T_IOTA + P

AR_AUG, AR_FV, AR_RQK, AR_RV = 0, 1056, 1568, 2592
AR_FT, AR_MQT, AR_PF, AR_PT = 3616, 5664, 6176, 8224
NAR = AR_PT + 1536
HEAD_AT = [0, 2, 1, 3]


def loads_of_trunk():
    out = [("kv", l, h) for l in range(DEPTH) for h in range(2)]
    for l in range(DEPTH):
        out += [("in", l, FQ, W, h) for h in range(2)]
        out += [("in", l, FV, QK + H, None), ("in", l, MQ, QK, None)]
        out += [("in", l, c, W, h) for c in (RQ, RV, RG) for h in range(2)]
        out += [("out", l, h) for h in range(4)]
        if l == 0:
            for c in range(NCH):
                out += [("gate", c, h) for h in range(2)]
                down = [("down", c - 1, h) for h in range(2) if c]
                up = [("up", c, h) for h in range(2)]
                out += up + down if c == NCH - 1 else down + up
            out += [("down", NCH - 1, h) for h in range(2)]
    return out


LOADS = loads_of_trunk()
MOE0 = len(LOADS)
MOE_LOADS = E_ * NCH * LPC
LAYER_LOADS = 14
KV0, IN0 = 0, 4
DENSE0 = IN0 + LAYER_LOADS
IN1 = DENSE0 + NCH * LPC


def build(nc, x, mem, w_in, w_mem_kv, w_out, dwg, dwu, dwd, ewg, ewu, ewd, par, tab, out):
    with ExitStack() as ctx:
        def sb(name, shape, dt=F32):
            return ctx.enter_context(nc.sbuf_tensor(name, shape, dt))

        sems = {}

        def sem(name):
            if name not in sems:
                sems[name] = ctx.enter_context(nc.semaphore("s_" + name))
            return sems[name]

        raw = sb("raw", [P, RAW, SLOT])
        whi = sb("whi", [P, SPLIT, SLOT], F32R)
        wlo = sb("wlo", [P, SPLIT, SLOT], F32R)
        xres = sb("xres", [P, NB, D])
        tok = sb("tok", [P, NB, D])
        sthi = sb("sthi", [P, NB, KT, P], F32R)
        stlo = sb("stlo", [P, NB, KT, P], F32R)
        hidhi = sb("hidhi", [P, NB, 4, P], F32R)
        hidlo = sb("hidlo", [P, NB, 4, P], F32R)
        scaled = sb("scaled", [P, 2, W])
        mkT = sb("mkT", [P, DEPTH, 2, SEQ])
        mval = sb("mval", [P, DEPTH, NB, QK])
        prm = sb("prm", [P, NPAR])
        tb = sb("tb", [P, NTAB])
        rthi = sb("rthi", [P, KT, E_], F32R)
        rtlo = sb("rtlo", [P, KT, E_], F32R)
        st = sb("st", [P, 128])
        guess = sb("guess", [P, 16], I32)
        newton = sb("newton", [P, 16])
        row_scale = sb("row_scale", [P, NB])
        sum_sq = sb("sum_sq", [P, NB])
        mem_scale = sb("mem_scale", [P, NB])
        rot = sb("rot", [P, 2, NB, 32])
        idb = sb("idb", [P, P], BF16)
        maskb = sb("maskb", [P, P], BF16)
        sel = sb("sel", [P, NB, E_])
        comb = sb("comb", [P, NB, E_])
        slot_of = sb("slot_of", [P, NB, 2 * E_ + 1])
        mx = sb("mx", [P, NB, 8])
        mi = sb("mi", [P, NB, 8], U32)
        mif = sb("mif", [P, NB, 8])
        flag = sb("flag", [P, 1], I32)
        ps = ctx.enter_context(nc.psum_tensor("ps", [P, 8, W], F32))

        with nc.sbuf_tensor("arena", [P, NAR], F32) as arena:
            pass
        sil = sb("sil", [P, NB, W])
        hid = sb("hid", [P, NB, W])
        onehot = sb("onehot", [P, NB, P], F32R)
        onehotT = sb("onehotT", [P, 2, NB, P], F32R)
        outhi, outlo = (sb(f"out{part_}", [P, D], F32R) for part_ in ("hi", "lo"))
        tokhi, toklo = (sb(f"tok{part_}", [P, NB, D], F32R) for part_ in ("hi", "lo"))

        ident = tb[:, T_ID:T_ID + P]
        tri = tb[:, T_TRI:T_TRI + P]
        ones = tb[:, T_ONE:T_ONE + P]
        decay = tb[:, T_DEC:T_DEC + 4 * SEQ].rearrange("p (h i) -> p h i", h=4)
        cos = tb[:, T_COS:T_COS + NB * 32].rearrange("p (b i) -> p b i", b=NB)
        sin = tb[:, T_SIN:T_SIN + NB * 32].rearrange("p (b i) -> p b i", b=NB)

        def ar(at, n):
            return arena[:, at:at + n]

        aug = ar(AR_AUG, 1056).rearrange("p (b h d) -> p b h d", b=NB, h=2 * H)
        fval = ar(AR_FV, 512).rearrange("p (b d) -> p b d", b=NB)
        rqk = ar(AR_RQK, 1024).rearrange("p (b d) -> p b d", b=NB)
        rval = ar(AR_RV, 1024).rearrange("p (b d) -> p b d", b=NB)
        fT = ar(AR_FT, 2048).rearrange("p (h t) -> p h t", h=2 * H)
        mqT = ar(AR_MQT, 512).rearrange("p (c t) -> p c t", c=2)
        rT = ar(AR_AUG, 1024).rearrange("p (c t) -> p c t", c=4)
        pf0 = ar(AR_PF, 512).rearrange("p (h t) -> p h t", h=4)
        pf1 = ar(AR_PF + 512, 1024).rearrange("p (h t) -> p h t", h=4)
        fpT0 = ar(AR_PT, 512).rearrange("p (h t) -> p h t", h=4)
        fpT1 = ar(AR_PT + 512, 1024).rearrange("p (h t) -> p h t", h=8)
        pm = [ar(AR_PF + 1024 * b, 1024).rearrange("p (h t) -> p h t", h=4) for b in range(NB)]
        mpT = [ar(AR_FT + 1024 * b, 1024).rearrange("p (h t) -> p h t", h=8) for b in range(NB)]
        rpT0 = ar(AR_PT, 1024).rearrange("p (h t) -> p h t", h=4)
        rpT1 = ar(AR_PT + 1024, 512).rearrange("p (h t) -> p h t", h=4)
        sq_early = ar(AR_PF, 1024).rearrange("p (b d) -> p b d", b=NB)
        mem_rows = [ar(at, 512).rearrange("p (b d) -> p b d", b=NB) for at in (NAR - 512, AR_PT)]
        logf = st[:, 64:72].rearrange("p (b h) -> p b h", b=NB)
        yret = tok[:, :, 0:512]
        yfox = tok[:, :, 512:768]
        ymem = tok[:, :, 768:1024]

        block = ctx.enter_context(nc.Block())

        def views(n):
            kind = LOADS[n]
            k, cols = {"kv": (4, W), "out": (2, D)}.get(kind[0], (None, None))
            if kind[0] == "in":
                k, cols = (8, kind[3]) if kind[4] is None else (4, W)
            return k, cols

        def part(t, slot, k, cols, rows=P):
            return t[0:rows, slot, 0:k * cols].rearrange("p (k n) -> p k n", k=k)

        def ffn_shape(kind, c, h):
            if kind != "down":
                return P, 4, CH[c]
            rest = 2 * P if h == 0 else CH[c] - 2 * P
            return min(P, rest), max(1, rest // P), D

        def ffn_source(wg, wu, wd, kind, c, h):
            if kind == "down":
                rows, k, _ = ffn_shape(kind, c, h)
                r0 = C0[c] + h * 2 * P
                return wd[r0:r0 + rows * k, :].rearrange("(k p) n -> p k n", p=rows)
            w = wg if kind == "gate" else wu
            return w[h * 512:(h + 1) * 512, C0[c]:C0[c] + CH[c]].rearrange("(k p) n -> p k n", p=P)

        def shape_of(n):
            if LOADS[n][0] in ("gate", "up", "down"):
                return ffn_shape(*LOADS[n])
            return (P, *views(n))

        def source_of(n):
            kind = LOADS[n]
            if kind[0] == "kv":
                return w_mem_kv[kind[1], kind[2] * 512:(kind[2] + 1) * 512, :].rearrange("(k p) n -> p k n", p=P)
            if kind[0] == "out":
                return w_out[kind[1], kind[2] * 256:(kind[2] + 1) * 256, :].rearrange("(k p) n -> p k n", p=P)
            if kind[0] == "in":
                _, l, c, n_, h = kind
                r0, r1 = (0, D) if h is None else (h * 512, (h + 1) * 512)
                return w_in[l, r0:r1, c:c + n_].rearrange("(k p) n -> p k n", p=P)
            return ffn_source(dwg[0], dwu[0], dwd[0], *kind)

        def moe_order(first):
            return [("gate", 0), ("gate", 1), ("up", 0), ("up", 1)] + ([] if first else [("down", 0), ("down", 1)])

        PAIR = 2 * NCH * LPC

        def first_of(it, par, c):
            return isinstance(it, int) and par == 0 and c == 0

        def moe_number(rnd, it, par, c, j):
            base = MOE0 + rnd * MOE_LOADS + par * NCH * LPC + c * LPC + j
            return base if first_of(it, par, c) else base - 2

        def counted(n, it, per=PAIR):
            return it * per + n

        def landed(eng, n, it=0):
            eng.wait_ge(sem(f"landed{n % RAW}"), counted(16 * (n // RAW + 1), it, PAIR // RAW * 16))

        def used(eng, n, it=0):
            eng.wait_ge(sem("weights_used"), counted(n + 1, it))

        def split_hi(eng, n, shape, it=0):
            landed(eng, n, it)
            if n >= SPLIT:
                used(eng, n - SPLIT, it)
            rows, k, cols = shape
            eng.activation(whi[0:rows, n % SPLIT, 0:k * cols], raw[0:rows, n % RAW, 0:k * cols],
                           ACT.Copy).then_inc(sem("hi_ready"), 1)

        def split_lo(eng, n, shape, it=0):
            eng.wait_ge(sem("hi_ready"), counted(n + 1, it))
            rows, k, cols = shape
            eng.tensor_tensor(wlo[0:rows, n % SPLIT, 0:k * cols], raw[0:rows, n % RAW, 0:k * cols],
                              whi[0:rows, n % SPLIT, 0:k * cols].bitcast(F32), ALU.subtract)\
                .then_inc(sem("lo_ready"), 1)

        def fetch(eng, n, src, shape, it=0):
            rows, k, cols = shape
            if n >= RAW:
                eng.wait_ge(sem("lo_ready"), counted(n - RAW + 1, it))
            eng.dma_start(part(raw, n % RAW, k, cols, rows), src).then_inc(sem(f"landed{n % RAW}"), 16)

        def ahead(split, eng, n):
            if n + SPLIT < MOE0 + SPLIT:
                split(eng, n + SPLIT, shape_of(n + SPLIT) if n + SPLIT < MOE0 else (P, 4, W))

        def moe_stages(rnd, it):
            out = []
            for par in range(2):
                for c in range(NCH):
                    for j, (kind, h) in enumerate(moe_order(first_of(it, par, c))):
                        out.append((par, c, j, moe_number(rnd, it, par, c, j),
                                    ffn_shape(kind, (c - 1) % NCH if kind == "down" else c, h)))
            return out

        def split_pair(split, eng, rnd, it, after):
            loads = moe_stages(rnd, it)
            if not (isinstance(it, int) and rnd == 0):
                for _, _, _, n, shape in loads[:SPLIT]:
                    split(eng, n, shape, it)
            for i, (par, c, j, n, _) in enumerate(loads):
                after(par, c, moe_order(first_of(it, par, c))[j], n)
                if i + SPLIT < len(loads):
                    split(eng, loads[i + SPLIT][3], loads[i + SPLIT][4], it)

        FLUSH = [ffn_shape("down", NCH - 1, h) for h in range(2)]

        TURNS = {"mem0": 0, "mem1": 1, "att0": 2, "out0": 3, "ffn0": 4, "att1": 5, "out1": 6, "ffn1": 7}
        TURNED = {name: i for i, name in enumerate(n for n in TURNS if n != "mem1")}
        X_ADDED = {"ffn0": 0, "att1": NB, "ffn1": 2 * NB}
        SCALED = {"att0": 0, "ffn0": 1, "att1": 2, "ffn1": 3}
        UNITS = [(u % NB, u // NB) for u in range(2 * NB)]

        def turn_bank(name, u):
            return (0 if name == "att1" else 4) + u

        def stationary(name):
            if name != "mem1":
                return sthi, stlo
            return (t[:, :, :].rearrange("p b (k t) -> p b k t", k=KT) for t in (tokhi, toklo))
        GAIN = {"mem0": G_MEM, "mem1": G_MEM + KT, "att0": G_ATT, "att1": G_ATT + KT, "out0": G_OUT,
                "out1": G_OUT + KT, "ffn0": G_FFN, "ffn1": G_FFN + KT}
        SQ = {name: i for i, name in enumerate(
            ("fqk0", "mq0", "mk", "fo0", "ro0", "mo0", "fqk1", "mq1", "fo1", "ro1", "mo1"))}
        DENSE_UNITS = NB * NCH

        @block.sync
        def _(sp):
            sp.dma_start(tb[:, T_ID:T_ID + P], tab[:, T_ID:T_ID + P]).then_inc(sem("ident_in"), 16)
            for b in range(NB):
                sp.dma_start(tok[:, b, :], mem[0, b * P:(b + 1) * P, :]).then_inc(sem(f"mem_in{b}"), 16)
                if b == 0:
                    sp.dma_start(prm[:, :], par).then_inc(sem("params"), 16)
            for n in range(MOE0):
                fetch(sp, n, source_of(n), shape_of(n))
                if n == 1:
                    sp.dma_start(xres[:, :, :], x[0].rearrange("(b p) d -> p b d", p=P)).then_inc(sem("x_in"), 16)
                if n == 4:
                    sp.dma_start(tb[:, T_ID + P:], tab[:, T_ID + P:]).then_inc(sem("tables"), 16)

            def fetch_pair(rnd, it):
                for par in range(2):
                    for c in range(NCH):
                        for j, (kind, h) in enumerate(moe_order(first_of(it, par, c))):
                            cc = c - 1 if kind == "down" else c
                            e = it * 2 + par - (1 if cc < 0 else 0)
                            cc %= NCH
                            fetch(sp, moe_number(rnd, it, par, c, j),
                                  ffn_source(expert(ewg, e), expert(ewu, e), expert(ewd, e), kind, cc, h),
                                  ffn_shape(kind, cc, h), it)

            def expert(w, e):
                if isinstance(e, int):
                    return w[0, e]
                return w[0, bass.ds(e, 1)].rearrange("a r n -> (a r) n")

            def fetch_round(rnd):
                fetch_pair(rnd, 0)
                with sp.Fori(1, E_ // 2) as it:
                    fetch_pair(rnd, it)
                for h in range(2):
                    fetch(sp, MOE0 + (rnd + 1) * MOE_LOADS - 2 + h,
                          ffn_source(None, None, ewd[0, E_ - 1], "down", NCH - 1, h), FLUSH[h])

            def store(rnd):
                for b in range(NB):
                    sp.wait_ge(sem("scatter_added"), 2 * E_ * (rnd + 1) - 1 + b)
                    sp.dma_start(out[0, b * P:(b + 1) * P, :], xres[:, b, :]).then_inc(sem("stored"), 16)

            fetch_round(0)
            sp.wait_ge(sem("flag_ready"), 1)
            with sp.If(sp.value_load(flag[0:1, 0:1], min_val=0, max_val=1) > 0):
                fetch_round(1)
                store(1)
            with sp.Else():
                store(0)
            sp.wait_ge(sem("stored"), NB * 16)

        @block.tensor
        def _(pe):
            def product(dst, rows, lhs, n, k, nk, cols, c0, c1, start, stop):
                xh, xl = lhs
                wh = part(whi, n % SPLIT, nk, cols, rows)[:, k, c0:c1]
                wl = part(wlo, n % SPLIT, nk, cols, rows)[:, k, c0:c1]
                pe.matmul(dst, xh, wh, start=start, stop=False)
                pe.matmul(dst, xh, wl, start=False, stop=False)
                return pe.matmul(dst, xl, wh, start=False, stop=stop)

            def stat(b, k):
                return sthi[:, b, k, :], stlo[:, b, k, :]

            def turn(name, units=range(4)):
                for u in units:
                    b, half = UNITS[u]
                    src = xres if name in X_ADDED or name == "att0" else tok
                    if name == "mem0":
                        pe.wait_ge(sem(f"mem_in{b}"), 16)
                    elif name == "att0":
                        pe.wait_ge(sem("x_in"), 16)
                        pe.wait_ge(sem("turn_scaled"), 4 * TURNS["mem1"] + u + 1)
                    elif name in X_ADDED:
                        pe.wait_ge(sem("x_added"), X_ADDED[name] + b + 1)
                    elif half == 0:
                        pe.wait_ge(sem("ret_rows"), NB * int(name[-1]) + b + 1)
                    else:
                        pe.wait_ge(sem("mem_rows"), NB * int(name[-1]) + b + 1)
                    for k in range(4):
                        d0 = (half * 4 + k) * P
                        last = pe.transpose(ps[:, turn_bank(name, u), k * P:(k + 1) * P], src[:, b, d0:d0 + P], ident)
                    last.then_inc(sem("turned"), 1)

            def turned_in(name, u):
                pe.wait_ge(sem("turn_lo"), 4 * TURNS[name] + u + 1)

            def project(n, bank, cols, halves, fresh=None):
                nk = KT // halves
                hi, lo = stationary(fresh)
                for h in range(halves):
                    pe.wait_ge(sem("lo_ready"), n + h + 1)
                    for b in range(NB):
                        if fresh:
                            turned_in(fresh, NB * h + b)
                        for k in range(nk):
                            kk = h * nk + k
                            last = product(ps[:, bank + b, 0:cols], P, (hi[:, b, kk, :], lo[:, b, kk, :]), n + h, k, nk, cols,
                                           0, cols, start=(h == 0 and k == 0), stop=(h == halves - 1 and k == nk - 1))
                    last.then_inc(sem("weights_used"), 1)

            def transposes(dst, tiles):
                for i, t in enumerate(tiles):
                    last = pe.transpose(dst(i), t, ident)
                return last

            pe.wait_ge(sem("ident_in"), 16)
            turn("mem0")
            project(KV0, 0, W, 2, "mem0")
            turn("att0")
            project(KV0 + 2, 2, W, 2, "mem1")

            def mixer(l, n):
                v = l + 1
                if l == 0:
                    pe.wait_ge(sem("kv_copied"), 1)
                project(n, 0, W, 2, f"att{l}")
                if l == 0:
                    pe.wait_ge(sem("kv_copied"), DEPTH)
                project(n + 2, 2, QK + H, 1)
                project(n + 3, 6, QK, 1)
                pe.wait_ge(sem("fv_copied"), v)
                project(n + 4, 2, W, 2)

                pe.wait_ge(sem("logf"), v)
                pe.wait_ge(sem("tables"), 16)
                sum0, sum1 = ps[:, 4, 0:4], ps[:, 4, 4:8]
                pe.matmul(sum0, tri, logf[:, 0], start=True, stop=True)
                pe.matmul(sum1, tri, logf[:, 1], start=True, stop=False)
                pe.matmul(sum1, ones, logf[:, 0], start=False, stop=True).then_inc(sem("logf_summed"), 1)
                pe.wait_ge(sem("fqk_rows"), v)
                project(n + 6, 0, W, 2)
                pe.wait_ge(sem("aug_ready"), v)
                pe.wait_ge(sem("mq_rows"), v)
                transposes(lambda i: ps[0:66, 4 + i // 4, (i % 4) * P:(i % 4 + 1) * P],
                           [aug[:, b, h, :] for h in range(2 * H) for b in range(NB)]).then_inc(sem("f_turned"), 1)
                pe.wait_ge(sem("r_rotated"), v)
                transposes(lambda i: ps[:, 2 + i // 4, (i % 4) * P:(i % 4 + 1) * P],
                           [rqk[:, b, c * P:(c + 1) * P] for c in range(4) for b in range(NB)])\
                    .then_inc(sem("r_turned"), 1)
                pe.wait_ge(sem("f_T"), 2 * v)
                pe.wait_ge(sem("mask_ready"), 2)
                for b in range(NB):
                    nk = (b + 1) * P
                    for h in range(H):
                        dst = ps[:, 4, h * P:(h + 1) * P] if b == 0 else ps[:, 5 + h // 2, (h % 2) * SEQ:(h % 2) * SEQ + nk]
                        pe.matmul(dst, fT[0:66, h, b * P:(b + 1) * P], fT[0:66, H + h, 0:nk], start=True, stop=False)
                        last = pe.matmul(dst[:, b * P:nk], idb[:, :], maskb[:, :], start=False, stop=True)
                    last.then_inc(sem("f_scored"), 1)
                transposes(lambda i: ps[:, 7, i * P:(i + 1) * P],
                           [ymem[:, b, c * P:(c + 1) * P] for c in range(2) for b in range(NB)])\
                    .then_inc(sem("mq_turned"), 1)
                pe.wait_ge(sem("rv_copied"), v)
                project(n + 8, 0, W, 2)
                if l == 0:
                    pe.wait_ge(sem("mk_normed"), 1)
                    pe.wait_ge(sem("r_T"), v)
                    for ll in range(DEPTH):
                        last = transposes(lambda i: ps[:, 2 + ll, i * P:(i + 1) * P],
                                          [mem_rows[ll][:, b, c * P:(c + 1) * P] for c in range(2) for b in range(NB)])
                    last.then_inc(sem("mk_turned"), 1)
                pe.wait_ge(sem("f_exp"), NB * l + 1)
                transposes(lambda i: ps[:, 4, i * P:(i + 1) * P], [pf0[:, h, :] for h in range(H)])\
                    .then_inc(sem("f_pturned"), 1)
                pe.wait_ge(sem("f_exp"), NB * l + 2)
                transposes(lambda i: ps[:, 5 + i // 4, (i % 4) * P:(i % 4 + 1) * P],
                           [pf1[:, h, j * P:(j + 1) * P] for h in range(H) for j in range(NB)])\
                    .then_inc(sem("f_pturned"), 1)

                def head_rows(h):
                    return slice(DH * (h % 2), DH * (h % 2) + DH)

                def mem_scores(b, bank):
                    for h in range(H):
                        r = head_rows(h)
                        last = pe.matmul(ps[:, bank + h % 2, (h // 2) * SEQ:(h // 2 + 1) * SEQ],
                                         mqT[r, h // 2, b * P:(b + 1) * P], mkT[r, l, h // 2, :], start=True, stop=True)
                    last.then_inc(sem("m_scored"), 1)

                pe.wait_ge(sem("r_T"), v)
                pe.wait_ge(sem("mk_T"), 1)
                pe.wait_ge(sem("mq_T"), v)
                mem_scores(0, 2)
                pe.wait_ge(sem("gate_silu"), v)
                for h in range(RH):
                    r = head_rows(h)
                    last = pe.matmul(ps[:, h % 2, (h // 2) * SEQ:(h // 2 + 1) * SEQ], rT[r, 2 + h // 2, 0:P],
                                     rT[r, h // 2, :], start=True, stop=True)
                last.then_inc(sem("r_scored"), 1)
                pe.wait_ge(sem("f_pT"), NB * v)
                for b in range(NB):
                    for h in range(H):
                        dst = ps[:, 7, b * QK + h * DH:b * QK + (h + 1) * DH]
                        for j in range(b + 1):
                            last = pe.matmul(dst, fpT0[:, h, :] if b == 0 else fpT1[:, 2 * h + j, :],
                                             fval[:, j, h * DH:(h + 1) * DH], start=(j == 0), stop=(j == b))
                last.then_inc(sem("f_valued"), 1)
                mem_scores(1, 4)
                pe.wait_ge(sem("f_out"), v)
                for h in range(RH):
                    r = head_rows(h)
                    last = pe.matmul(ps[:, 6 + h % 2, (h // 2) * P:(h // 2 + 1) * P], rT[r, 2 + h // 2, P:SEQ],
                                     rT[r, h // 2, P:SEQ], start=True, stop=True)
                last.then_inc(sem("r_scored"), 1)
                pe.wait_ge(sem("r_decayed"), 2 * v)
                for b in range(NB):
                    for h in range(RH):
                        a = HEAD_AT[h]
                        dst = ps[:, b, h * RDV:(h + 1) * RDV]
                        last = pe.matmul(dst, rpT0[:, a, b * P:(b + 1) * P], rval[:, 0, h * RDV:(h + 1) * RDV],
                                         start=True, stop=(b == 0))
                        if b:
                            last = pe.matmul(dst, rpT1[:, a, :], rval[:, 1, h * RDV:(h + 1) * RDV], start=False, stop=True)
                last.then_inc(sem("r_valued"), 1)
                for b in range(NB):
                    pe.wait_ge(sem("m_exp"), NB * l + b + 1)
                    transposes(lambda i: ps[:, 2 + 2 * b + i // 4, (i % 4) * P:(i % 4 + 1) * P],
                               [pm[b][:, HEAD_AT[h], j * P:(j + 1) * P] for h in range(H) for j in range(NB)])\
                        .then_inc(sem("m_pturned"), 1)
                pe.wait_ge(sem("m_pT"), NB * v)
                for b in range(NB):
                    for h in range(H):
                        dst = ps[:, 6, b * QK + h * DH:b * QK + (h + 1) * DH]
                        for j in range(NB):
                            last = pe.matmul(dst, mpT[b][:, 2 * h + j, :], mval[:, l, j, h * DH:(h + 1) * DH],
                                             start=(j == 0), stop=(j == NB - 1))
                last.then_inc(sem("m_valued"), 1)
                for q in range(4):
                    m = n + 10 + q
                    if q < 2:
                        turn(f"out{l}", (2 * q, 2 * q + 1))
                    pe.wait_ge(sem("lo_ready"), m + 1)
                    for b in range(NB):
                        turned_in(f"out{l}", NB * (q // 2) + b)
                        for k in range(2):
                            for half in range(2):
                                last = product(ps[:, 2 * b + half, :], P, stat(b, 2 * q + k), m, k, 2, D,
                                               half * W, (half + 1) * W, start=(q == 0 and k == 0), stop=(q == 3 and k == 1))
                        if q == 3 and b == 0:
                            last.then_inc(sem("block_summed"), 1)
                    last.then_inc(sem("weights_used"), 1)

            def widths(kind, n, it, c, h, nb, par, bank, unit, fresh=None):
                pe.wait_ge(sem("lo_ready"), counted(n + 1, it))
                for b in range(nb):
                    if fresh:
                        turned_in(fresh, NB * h + b)
                    if h == 0 and unit + b >= nb:
                        pe.wait_ge(sem("silu_done" if kind == "gate" else "hidden_ready"),
                                   counted(unit + b - nb + 1, it, 2 * NCH))
                    for k in range(4):
                        last = product(ps[:, bank + b, 0:CH[c]], P, stat(b if nb > 1 else par, 4 * h + k), n, k, 4,
                                       CH[c], 0, CH[c], start=(h == 0 and k == 0), stop=(h == 1 and k == 3))
                last.then_inc(sem("weights_used"), 1)

            def turn_hidden(it, c, nb, bank, unit):
                for b in range(nb):
                    pe.wait_ge(sem("hidden_ready"), counted(unit + b + 1, it, 2 * NCH))
                    if unit + b >= nb:
                        pe.wait_ge(sem("hid_lo"), counted(unit + b - nb + 1, it, 2 * NCH))
                    for k in range(-(-CH[c] // P)):
                        f = min(P, CH[c] - k * P)
                        last = pe.transpose(ps[0:f, bank + b, k * P:(k + 1) * P], hid[:, b, k * P:k * P + f], ident)
                    last.then_inc(sem("hid_turned"), 1)

            def down(n, it, c, h, nb, unit, start, stop):
                pe.wait_ge(sem("lo_ready"), counted(n + 1, it))
                rows, nk, _ = ffn_shape("down", c, h)
                for b in range(nb):
                    if h == 0:
                        pe.wait_ge(sem("hid_lo"), counted(unit + b + 1, it, 2 * NCH))
                    for k in range(nk):
                        kk = 2 * h + k
                        for half in range(2):
                            last = product(ps[:, 4 + 2 * b + half, :], rows,
                                           (hidhi[0:rows, b, kk, :], hidlo[0:rows, b, kk, :]), n, k, nk, D,
                                           half * W, (half + 1) * W, start=(start and h == 0 and k == 0),
                                           stop=(stop and h == 1 and k == nk - 1))
                    if stop and h == 1 and b < nb - 1:
                        last.then_inc(sem("block_summed"), 1)
                last.then_inc(sem("weights_used"), 1)

            mixer(0, IN0)
            turn("ffn0")
            n = DENSE0
            for c in range(NCH):
                fresh = "ffn0" if c == 0 else None
                widths("gate", n, 0, c, 0, NB, 0, 0, NB * c, fresh)
                if c:
                    turn_hidden(0, c - 1, NB, 2, NB * (c - 1))
                widths("gate", n + 1, 0, c, 1, NB, 0, 0, NB * c, fresh)
                n += 2
                if 0 < c < NCH - 1:
                    for h in range(2):
                        down(n + h, 0, c - 1, h, NB, NB * (c - 1), c == 1, False)
                    n += 2
                if c == NCH - 1:
                    pe.wait_ge(sem("hid_lo"), NB * c)
                for h in range(2):
                    widths("up", n + h, 0, c, h, NB, 0, 2, NB * c)
                n += 2
            down(n, 0, NCH - 2, 0, NB, NB * (NCH - 2), False, False)
            turn_hidden(0, NCH - 1, NB, 2, NB * (NCH - 1))
            down(n + 1, 0, NCH - 2, 1, NB, NB * (NCH - 2), False, False)
            n += 2
            for h in range(2):
                down(n + h, 0, NCH - 1, h, NB, NB * (NCH - 1), False, True)

            turn("att1")
            mixer(1, IN1)
            turn("ffn1")
            pe.wait_ge(sem("router_lo"), 1)
            for k in range(KT):
                if k % (KT // 2) == 0:
                    for b in range(NB):
                        turned_in("ffn1", NB * (k // (KT // 2)) + b)
                dst = ps[0:E_, 0, 0:SEQ].rearrange("e (b t) -> e b t", b=NB)
                pe.matmul(dst, rthi[:, k, :], sthi[:, :, k, :], start=(k == 0), stop=False)
                pe.matmul(dst, rtlo[:, k, :], sthi[:, :, k, :], start=False, stop=False)
                last = pe.matmul(dst, rthi[:, k, :], stlo[:, :, k, :], start=False, stop=(k == KT - 1))
            last.then_inc(sem("logits_summed"), 1)
            pe.wait_ge(sem("logits_copied"), 1)
            for b in range(NB):
                last = pe.transpose(ps[:, 1, b * E_:(b + 1) * E_], hid[0:E_, 0, b * P:(b + 1) * P], ident[0:E_, 0:E_])
            last.then_inc(sem("logits"), 1)
            pe.wait_ge(sem("chosen"), 1)
            upto0, upto1, total = (ps[:, 7, i * E_:(i + 1) * E_] for i in range(3))
            pe.matmul(upto0, tri, sel[:, 0], start=True, stop=True)
            pe.matmul(upto1, tri, sel[:, 1], start=True, stop=False)
            pe.matmul(upto1, ones, sel[:, 0], start=False, stop=True)
            pe.matmul(total, ones, sel[:, 0], start=True, stop=False)
            pe.matmul(total, ones, sel[:, 1], start=False, stop=True).then_inc(sem("ranked"), 1)

            def turn_onehot(k, it):
                pe.wait_ge(sem("onehot_ready"), counted(k + 1, it, 2))
                if k:
                    pe.wait_ge(sem("gathered_scaled"), counted(2 * k, it, 4))
                transposes(lambda b: ps[:, 3, b * P:(b + 1) * P], [onehot[:, b, :].bitcast(F32) for b in range(NB)])\
                    .then_inc(sem("onehot_turned"), 1)

            def collect(k, it, half, bank=3):
                if k == 0 and isinstance(it, int):
                    pe.wait_ge(sem("onehot_ready"), 1)
                elif half == 0:
                    pe.wait_ge(sem("onehot_T"), counted(k + 1, it, 2))
                else:
                    pe.wait_ge(sem("rows_copied"), counted(2 * k + 1, it, 4))
                cols = slice(half * W, (half + 1) * W)
                for b in range(NB):
                    pe.matmul(ps[:, bank, :], onehot[:, b, :], tokhi[:, b, cols], start=(b == 0), stop=False)
                    last = pe.matmul(ps[:, bank, :], onehot[:, b, :], toklo[:, b, cols], start=False, stop=(b == NB - 1))
                last.then_inc(sem("collected"), 1)

            def gather(k, it, half, bank=3):
                if k == 0 and isinstance(it, int):
                    pe.wait_ge(sem("rows_copied"), half + 1)
                elif half == 0:
                    pe.wait_ge(sem("rows_copied"), counted(2 * k + 2, it, 4))
                else:
                    pe.wait_ge(sem("gathered_scaled"), counted(2 * k + 1, it, 4))
                transposes(lambda t: ps[:, bank, t * P:(t + 1) * P],
                           [tok[:, 0, (4 * half + t) * P:(4 * half + t + 1) * P] for t in range(4)])\
                    .then_inc(sem("gathered"), 1)

            def scatter(k, it, par, b, banks=6):
                pe.wait_ge(sem("out_copied"), counted(k + 1, it, 2))
                if banks != 6:
                    pe.wait_ge(sem("hidden_ready"), DENSE_UNITS + (k + 1) * NCH)
                    pe.wait_ge(sem("gathered_scaled"), 2 * (k + 2))
                elif 2 * k + b:
                    pe.wait_ge(sem("scatter_added"), counted(2 * k + b, it, 4))
                for half in range(2):
                    cols = slice(half * W, (half + 1) * W)
                    pe.matmul(ps[:, banks + half, :], onehotT[:, par, b, :], outhi[:, cols], start=True, stop=False)
                    last = pe.matmul(ps[:, banks + half, :], onehotT[:, par, b, :], outlo[:, cols], start=False, stop=True)
                last.then_inc(sem("scattered"), 1)

            def expert_pair(rnd, it):
                for par in range(2):
                    k = rnd * E_ + par
                    before = not (isinstance(it, int) and par == 0)
                    for c in range(NCH):
                        u = DENSE_UNITS + k * NCH + c
                        def at(j):
                            return moe_number(rnd, it, par, c, j)
                        for h in range(2):
                            if c == 0:
                                pe.wait_ge(sem("gathered_lo"), counted(2 * k + h + 1, it, 4))
                            widths("gate", at(h), it, c, h, 1, par, 0, u)
                        if c or before:
                            turn_hidden(it, (c - 1) % NCH, 1, 1, u - 1)
                        if c == 2:
                            if before:
                                scatter(k - 1, it, 1 - par, 1)
                            turn_onehot(k + 1, it)
                        for h in range(2):
                            widths("up", at(2 + h), it, c, h, 1, par, 2, u)
                        if c == 1 and before:
                            scatter(k - 1, it, 1 - par, 0)
                        if c in (2, 3):
                            collect(k + 1, it, c - 2)
                        if c == 4:
                            gather(k + 1, it, 0)
                        if c == 1 and (k or not isinstance(it, int)):
                            pe.wait_ge(sem("out_copied"), counted(k, it, 2))
                        if c or before:
                            for h in range(2):
                                down(at(4 + h), it, (c - 1) % NCH, h, 1, u - 1, c == 1, c == 0)
                        if c == 4:
                            gather(k + 1, it, 1)

            def expert_round(rnd):
                if rnd:
                    pe.wait_ge(sem("scatter_added"), 2 * rnd * E_)
                expert_pair(rnd, 0)
                with pe.Fori(1, E_ // 2) as it:
                    expert_pair(rnd, it)
                u = DENSE_UNITS + (rnd + 1) * E_ * NCH - 1
                turn_hidden(0, NCH - 1, 1, 1, u)
                for h in range(2):
                    down(MOE0 + (rnd + 1) * MOE_LOADS - 2 + h, 0, NCH - 1, h, 1, u, False, True)
                for b in range(NB):
                    scatter((rnd + 1) * E_ - 1, 0, 1, b, (6, 2)[b])

            pe.wait_ge(sem("rows_split"), 1)
            for half in range(2):
                collect(0, 0, half, 3 - half)
            for half in range(2):
                gather(0, 0, half, 3 - half)
            pe.wait_ge(sem("gathered_scaled"), 1)
            turn_onehot(0, 0)
            expert_round(0)
            pe.wait_ge(sem("flag_ready"), 1)
            with pe.If(pe.value_load(flag[0:1, 0:1], min_val=0, max_val=1) > 0):
                expert_round(1)
            with pe.Else():
                pe.nop()

        @block.scalar
        def _(act):
            own = [0]

            def then(ins):
                own[0] += 1
                ins.then_inc(sem("act_step"), 1)
                act.wait_ge(sem("act_step"), own[0])

            def step(n):
                ahead(split_hi, act, n)

            def turn(name, units=range(4)):
                hi, _ = stationary(name)
                for u in units:
                    b, half = UNITS[u]
                    act.wait_ge(sem("turn_scaled"), 4 * TURNS[name] + u + 1)
                    act.activation(hi[:, b, 4 * half:4 * half + 4, :].rearrange("p k t -> p (k t)"), scaled[:, u % 2, :],
                                   ACT.Copy).then_inc(sem("turn_hi"), 1)

            def by_row(dst, src, func, scales):
                for b in range(NB):
                    last = act.activation(dst[:, b], src[:, b], func, scale=scales[:, b:b + 1])
                return last

            def squares(name, dst, src, scales=None):
                if SQ[name]:
                    act.wait_ge(sem("sq_summed"), SQ[name])
                if scales is None:
                    act.activation(dst, src, ACT.Square).then_inc(sem("sq_done"), 1)
                else:
                    by_row(dst, src, ACT.Square, scales).then_inc(sem("sq_done"), 1)

            def memory_values(l):
                act.wait_ge(sem("mem_scale"), 1)
                used(act, KV0 + 2 * l + 1)
                by_row(mem_rows[l], ps[:, 2 * l:2 * l + 2, 0:QK], ACT.Copy, mem_scale)
                by_row(mval[:, l, :, :], ps[:, 2 * l:2 * l + 2, QK:2 * QK], ACT.Copy, mem_scale).then_inc(sem("kv_copied"), 1)

            def memory_squares():
                act.wait_ge(sem("kv_copied"), DEPTH)
                act.activation(scaled[:, :, 0:QK], mem_rows[0], ACT.Square)
                squares("mk", scaled[:, :, QK:2 * QK], mem_rows[1])

            turn("mem0")
            split_hi(act, 0, shape_of(0))
            split_hi(act, 1, shape_of(1))
            turn("mem1")
            split_hi(act, 2, shape_of(2))
            step(KV0)
            step(KV0 + 1)
            turn("att0")
            memory_values(0)
            step(KV0 + 2)
            step(KV0 + 3)
            memory_values(1)
            act.wait_ge(sem("params"), 16)
            act.activation(rthi[:, :, :].rearrange("p k e -> p (k e)"), prm[:, ROUT:ROUT + KT * E_], ACT.Copy)\
                .then_inc(sem("router_hi"), 1)

            def mixer(l, n):
                v = l + 1
                step(n)
                step(n + 1)
                act.wait_ge(sem("row_scale"), SCALED[f"att{l}"] + 1)
                squares(f"fqk{l}", sq_early[:, :, :], ps[:, 0:2, :], row_scale)
                step(n + 2)
                act.wait_ge(sem("z_ready"), v)
                then(act.activation(st[:, 88:96], st[:, 80:88], ACT.Exp, scale=-1.0))
                act.activation(st[:, 96:104], st[:, 88:96], ACT.Ln, bias=1.0).then_inc(sem("ln_done"), 1)
                step(n + 3)
                squares(f"mq{l}", sq_early[:, :, 0:QK], ps[:, 6:8, 0:QK], row_scale)
                if l == 0:
                    memory_squares()
                step(n + 4)
                step(n + 5)
                step(n + 6)
                act.wait_ge(sem("f_turned"), v)
                act.activation(fT[0:66, H:2 * H, :].rearrange("p h t -> p (h t)"),
                               ps[0:66, 6:8, :].rearrange("p c t -> p (c t)"), ACT.Copy,
                               scale=prm[0:66, G_FK + l:G_FK + l + 1]).then_inc(sem("f_T"), 1)
                act.wait_ge(sem("r_turned"), v)
                act.activation(rT.rearrange("p c t -> p (c t)"), ps[:, 2:4, :].rearrange("p c t -> p (c t)"), ACT.Copy)\
                    .then_inc(sem("r_T"), 1)
                by_row(rval[:, :, :], ps[:, 0:2, :], ACT.Copy, row_scale).then_inc(sem("rv_copied"), 1)

                def exps(b, src, dst, at, maxed, done):
                    act.wait_ge(sem(maxed), NB * l + b + 1)
                    for a in range(H):
                        c = at + b * H + a
                        last = act.activation(dst[:, a, :], src(a), ACT.Exp, bias=st[:, c:c + 1],
                                              accum_out=st[:, c + 8:c + 9])
                    last.then_inc(sem(done), 1)

                exps(0, lambda a: ps[:, 4, a * P:(a + 1) * P], pf0, 32, "f_max", "f_exp")
                exps(1, lambda a: ps[:, 5 + a // 2, (a % 2) * SEQ:(a % 2 + 1) * SEQ], pf1, 32, "f_max", "f_exp")
                step(n + 7)
                step(n + 8)
                used(act, n + 9)
                by_row(yret, ps[:, 0:2, :], ACT.Silu, row_scale).then_inc(sem("gate_silu"), 1)
                act.wait_ge(sem("f_pturned"), NB * l + 1)
                act.activation(fpT0.rearrange("p h t -> p (h t)"), ps[:, 4, :], ACT.Copy).then_inc(sem("f_pT"), 1)
                exps(0, lambda a: ps[:, 2 + a // 2, (a % 2) * SEQ:(a % 2 + 1) * SEQ], pm[0], 48, "m_max", "m_exp")
                step(n + 9)
                act.wait_ge(sem("f_out"), v)
                squares(f"fo{l}", scaled[:, :, 0:QK], yfox)
                exps(1, lambda a: ps[:, 4 + a // 2, (a % 2) * SEQ:(a % 2 + 1) * SEQ], pm[1], 48, "m_max", "m_exp")
                act.wait_ge(sem("r_valued"), v)
                squares(f"ro{l}", scaled[:, :, :], ps[:, 0:2, :])
                for b in range(NB):
                    act.wait_ge(sem("m_pturned"), NB * l + b + 1)
                    act.activation(mpT[b].rearrange("p h t -> p (h t)"),
                                   ps[:, 2 + 2 * b:4 + 2 * b, :].rearrange("p c t -> p (c t)"), ACT.Copy)\
                        .then_inc(sem("m_pT"), 1)
                turn(f"out{l}", (0, 1))
                act.wait_ge(sem("m_out"), v)
                squares(f"mo{l}", scaled[:, :, 0:QK], ymem)
                turn(f"out{l}", (2, 3))
                for q in range(3):
                    step(n + 10 + q)
                next_turn(f"ffn{l}", n + 13)

            def next_turn(name, n):
                def sum_squares(b):
                    act.wait_ge(sem("x_added"), X_ADDED[name] + b + 1)
                    return act.activation(tok[:, b, :], xres[:, b, :], ACT.Square, accum_out=sum_sq[:, b:b + 1])

                sum_squares(0)
                used(act, n)
                turn(name)
                sum_squares(1).then_inc(sem("x_squared"), 1)
                if n < MOE0 - 1:
                    step(n)

            def silus(it, c, nb, bank, unit):
                for b in range(nb):
                    if unit + b >= nb:
                        act.wait_ge(sem("hidden_ready"), counted(unit + b - nb + 1, it, 2 * NCH))
                    scale = row_scale[:, b:b + 1] if nb > 1 else 1.0
                    act.activation(sil[:, b, 0:CH[c]], ps[:, bank + b, 0:CH[c]], ACT.Silu, scale=scale)\
                        .then_inc(sem("silu_done"), 1)

            def hidden_hi(it, c, nb, bank, unit):
                for b in range(nb):
                    act.wait_ge(sem("hid_turned"), counted(unit + b + 1, it, 2 * NCH))
                    full, rest = CH[c] // P, CH[c] % P
                    last = act.activation(hidhi[:, b, 0:full, :].rearrange("p k t -> p (k t)"), ps[:, bank + b, 0:full * P],
                                          ACT.Copy)
                    if rest:
                        last = act.activation(hidhi[0:rest, b, full, :], ps[0:rest, bank + b, full * P:(full + 1) * P], ACT.Copy)
                    last.then_inc(sem("hid_hi"), 1)

            mixer(0, IN0)
            n = DENSE0
            act.wait_ge(sem("row_scale"), SCALED["ffn0"] + 1)
            for c in range(NCH):
                step(n)
                if c:
                    hidden_hi(0, c - 1, NB, 2, NB * (c - 1))
                used(act, n + 1)
                silus(0, c, NB, 0, NB * c)
                step(n + 1)
                for i in range(4 if 0 < c < NCH - 1 else 2):
                    step(n + 2 + i)
                n += LPC if 0 < c < NCH - 1 else 4
            step(n)
            used(act, n + 1)
            hidden_hi(0, NCH - 1, NB, 2, NB * (NCH - 1))
            step(n + 1)
            n += 2
            step(n)
            next_turn("att1", n + 1)
            mixer(1, IN1)
            act.wait_ge(sem("logits_summed"), 1)
            act.activation(hid[0:E_, 0, 0:SEQ], ps[0:E_, 0, 0:SEQ], ACT.Copy).then_inc(sem("logits_copied"), 1)
            act.wait_ge(sem("row_scale"), SCALED["ffn1"] + 1)
            by_row(tokhi[:, :, :], xres[:, :, :], ACT.Copy, row_scale).then_inc(sem("rows_hi"), 1)
            step(MOE0 - 1)
            act.wait_ge(sem("top_two"), 1)
            act.activation(st[:, 108:110], st[:, 106:108], ACT.Exp).then_inc(sem("gate_exp"), 1)

            def onehot_out(k, it, par):
                act.wait_ge(sem("onehot_turned"), counted(k + 1, it, 2))
                act.activation(onehotT[:, par, :, :].rearrange("p b t -> p (b t)"), ps[:, 3, 0:NB * P], ACT.Copy)\
                    .then_inc(sem("onehot_T"), 1)

            def rows_copy(k, it, half, bank=3):
                act.wait_ge(sem("collected"), counted(2 * k + half + 1, it, 4))
                if half == 0 and (k or not isinstance(it, int)):
                    act.wait_ge(sem("gathered"), counted(2 * k, it, 4))
                act.activation(tok[:, 0, half * W:(half + 1) * W], ps[:, bank, :], ACT.Copy).then_inc(sem("rows_copied"), 1)

            def gathered_hi(k, it, par, half):
                act.wait_ge(sem("gathered_scaled"), counted(2 * k + half + 1, it, 4))
                act.activation(sthi[:, par, 4 * half:4 * half + 4, :].rearrange("p k t -> p (k t)"), scaled[:, half, :],
                               ACT.Copy).then_inc(sem("gathered_hi"), 1)

            def out_copy(k, it):
                if k or not isinstance(it, int):
                    act.wait_ge(sem("scattered"), counted(2 * k, it, 4))
                act.activation(outhi[:, :], ps[:, 4:6, :].rearrange("p c n -> p (c n)"), ACT.Copy).then_inc(sem("out_hi"), 1)

            def expert_pair(rnd, it):
                def after(par, c, what, n):
                    k = rnd * E_ + par
                    u = DENSE_UNITS + k * NCH + c
                    before = not (isinstance(it, int) and par == 0)
                    if what in (("gate", 1), ("down", 1)) and (what[0] == "gate" or c == 0):
                        used(act, n, it)
                    if what == ("gate", 1):
                        silus(it, c, 1, 0, u)
                        if c or before:
                            hidden_hi(it, (c - 1) % NCH, 1, 1, u - 1)
                    if c == 2 and what == ("up", 0):
                        onehot_out(k + 1, it, 1 - par)
                    if what == ("down", 1) and c in (2, 3):
                        rows_copy(k + 1, it, c - 2)
                    if (c, what) in ((4, ("down", 1)), (5, ("up", 0))):
                        gathered_hi(k + 1, it, 1 - par, c - 4)
                    if what == ("down", 1) and c == 0:
                        out_copy(k - 1, it)
                split_pair(split_hi, act, rnd, it, after)

            def expert_round(rnd):
                expert_pair(rnd, 0)
                with act.Fori(1, E_ // 2) as it:
                    expert_pair(rnd, it)
                n0 = MOE0 + (rnd + 1) * MOE_LOADS - 2
                for h in range(2):
                    split_hi(act, n0 + h, FLUSH[h])
                hidden_hi(0, NCH - 1, 1, 1, DENSE_UNITS + (rnd + 1) * E_ * NCH - 1)
                used(act, n0 + 1)
                out_copy((rnd + 1) * E_ - 1, 0)

            for half in range(2):
                rows_copy(0, 0, half, 3 - half)
            for half in range(2):
                gathered_hi(0, 0, 0, half)
            onehot_out(0, 0, 0)
            expert_round(0)
            act.wait_ge(sem("flag_ready"), 1)
            with act.If(act.value_load(flag[0:1, 0:1], min_val=0, max_val=1) > 0):
                expert_round(1)
            with act.Else():
                act.nop()

        @block.vector
        def _(dve):
            own = [0]

            def then(ins):
                own[0] += 1
                ins.then_inc(sem("dve_step"), 1)
                dve.wait_ge(sem("dve_step"), own[0])

            def step(n):
                ahead(split_lo, dve, n)

            def flat(t):
                return t.rearrange("p k t -> p (k t)")

            def scale_unit(src, gain, half, dst, done):
                g = prm[:, gain + 4 * half:gain + 4 * half + 4].unsqueeze(2).to_broadcast([P, 4, P])
                dve.tensor_tensor(dst.rearrange("p (k t) -> p k t", k=4), src.rearrange("p (k t) -> p k t", k=4),
                                  g, ALU.mult).then_inc(sem(done), 1)

            def turn(name, units=range(4)):
                hi, low = stationary(name)

                def lo(u):
                    b, half = UNITS[u]
                    dve.wait_ge(sem("turn_hi"), 4 * TURNS[name] + u + 1)
                    dve.tensor_tensor(flat(low[:, b, 4 * half:4 * half + 4, :]), scaled[:, u % 2, :],
                                      flat(hi[:, b, 4 * half:4 * half + 4, :]).bitcast(F32), ALU.subtract)\
                        .then_inc(sem("turn_lo"), 1)
                for u in units:
                    g = 4 * TURNS[name] + u
                    dve.wait_ge(sem("turned"), 4 * TURNED.get(name, 0) + u + 1)
                    if g >= 2:
                        dve.wait_ge(sem("turn_lo"), g - 1)
                    scale_unit(ps[:, turn_bank(name, u), :], GAIN[name], UNITS[u][1], scaled[:, u % 2, :], "turn_scaled")
                    if u > units[0]:
                        lo(u - 1)
                lo(units[-1])

            def inverse_rms(n, width, y, x=None):
                x, t, h = st[:, 0:n] if x is None else x, guess[:, 0:n], newton[:, 0:n]
                then(dve.tensor_scalar(x, x, 1.0 / width, EPS, ALU.mult, ALU.add))
                then(dve.tensor_scalar(t, x.bitcast(I32), 1, None, ALU.logical_shift_right))
                then(dve.tensor_scalar(y.bitcast(I32), t, -1.0, float(0x5F3759DF), ALU.mult, ALU.add))
                then(dve.tensor_scalar(x, x, -0.5, None, ALU.mult))
                for i in range(3):
                    then(dve.tensor_tensor(h, y, y, ALU.mult))
                    then(dve.tensor_tensor(h, h, x, ALU.mult))
                    last = dve.scalar_tensor_tensor(out=y, in0=h, scalar=1.5, in1=y, op0=ALU.add, op1=ALU.mult)
                    if i < 2:
                        then(last)
                return last

            def row_scales(src, dst, done, count, after):
                dve.wait_ge(sem("turn_lo"), 4 * (TURNS[after] + 1))
                for b in range(NB):
                    then(dve.tensor_tensor_reduce(out=scaled[:, :, :].rearrange("p a n -> p (a n)"), in0=src[:, b, :],
                                                  in1=src[:, b, :], scale=1.0, scalar=0.0, op0=ALU.mult, op1=ALU.add,
                                                  accum_out=st[:, b:b + 1]))
                inverse_rms(NB, D, dst[:, :]).then_inc(sem(done), 1)
                dve.wait_ge(sem(done), count)

            def by_row(dst, src, scales):
                for b in range(NB):
                    last = dve.tensor_scalar(dst[:, b], src[:, b], scales[:, b:b + 1], None, ALU.mult)
                return last

            def head_scales(name, sq, width, hh, rows=None):
                dve.wait_ge(sem("sq_done"), SQ[name] + 1)
                dve.tensor_reduce(st[:, 0:NB * hh].rearrange("p (b h) -> p b h", b=NB),
                                  sq.rearrange("p b (h d) -> p b h d", d=width), AX.X, ALU.add)\
                    .then_inc(sem("sq_summed"), 1)
                dve.wait_ge(sem("sq_summed"), SQ[name] + 1)
                then(inverse_rms(NB * hh, width, st[:, 16:16 + NB * hh]))
                r = st[:, 16:16 + NB * hh].rearrange("p (b h) -> p b h", b=NB)
                if rows is not None:
                    then(dve.tensor_tensor(r, r, rows[:, :].unsqueeze(2).to_broadcast([P, NB, hh]), ALU.mult))
                return r

            def by_head(dst, src, scales, width):
                hh = scales.shape[2]
                return dve.tensor_tensor(dst if len(dst.shape) == 4 else dst.rearrange("p b (h d) -> p b h d", d=width),
                                         src.rearrange("p b (h d) -> p b h d", d=width),
                                         scales.unsqueeze(3).to_broadcast([P, NB, hh, width]), ALU.mult)

            def memory_keys():
                dve.wait_ge(sem("sq_done"), SQ["mk"] + 1)
                dve.tensor_reduce(st[:, 0:16].rearrange("p (l b h) -> p b l h", l=DEPTH, b=NB),
                                  scaled[:, :, :].rearrange("p b (l h d) -> p b l h d", l=DEPTH, d=DH), AX.X, ALU.add)\
                    .then_inc(sem("sq_summed"), 1)
                dve.wait_ge(sem("sq_summed"), SQ["mk"] + 1)
                then(inverse_rms(16, DH, st[:, 16:32]))
                for l in range(DEPTH):
                    r = st[:, 16 + 8 * l:24 + 8 * l].rearrange("p (b h) -> p b h", b=NB)
                    last = by_head(mem_rows[l], mem_rows[l], r, DH)
                last.then_inc(sem("mk_normed"), 1)

            def memory_turned():
                dve.wait_ge(sem("mk_turned"), 1)
                for l in range(DEPTH):
                    last = dve.tensor_scalar(flat(mkT[:, l, :, :]), ps[:, 2 + l, :], prm[:, G_MK + l:G_MK + l + 1], None,
                                             ALU.mult)
                last.then_inc(sem("mk_T"), 1)

            def next_turn(name, n, banks, late=None):
                count = (n == DENSE0 - 1, n == IN1 - 1, n == MOE0 - 1).index(True)
                for b in range(NB):
                    if b:
                        used(dve, n)
                    else:
                        dve.wait_ge(sem("block_summed"), count + 1)
                    at = banks + 2 * b
                    dve.tensor_tensor(xres[:, b, :], xres[:, b, :], flat(ps[:, at:at + 2, :]), ALU.add)\
                        .then_inc(sem("x_added"), 1)
                turn(name)
                if late is not None:
                    step(late)
                dve.wait_ge(sem("x_squared"), count + 1)
                inverse_rms(NB, D, row_scale[:, :], sum_sq[:, :]).then_inc(sem("row_scale"), 1)
                dve.wait_ge(sem("row_scale"), SCALED[name] + 1)
                if n < MOE0 - 1:
                    step(n)

            dve.wait_ge(sem("params"), 16)
            turn("mem0")
            split_lo(dve, 0, shape_of(0))
            split_lo(dve, 1, shape_of(1))
            turn("mem1")
            split_lo(dve, 2, shape_of(2))
            step(KV0)
            for b in range(NB):
                dve.wait_ge(sem(f"mem_in{b}"), 16)
            row_scales(tok, mem_scale, "mem_scale", 1, "mem1")
            step(KV0 + 1)
            turn("att0")
            dve.wait_ge(sem("x_in"), 16)
            row_scales(xres, row_scale, "row_scale", 1, "att0")
            step(KV0 + 2)
            step(KV0 + 3)
            dve.wait_ge(sem("tables"), 16)
            dve.tensor_copy(idb[:, :], ident).then_inc(sem("mask_ready"), 1)
            dve.tensor_copy(maskb[:, :], tb[:, T_MASK:T_MASK + P]).then_inc(sem("mask_ready"), 1)
            dve.wait_ge(sem("router_hi"), 1)
            dve.tensor_tensor(flat(rtlo[:, :, :]), prm[:, ROUT:ROUT + KT * E_], flat(rthi[:, :, :]).bitcast(F32),
                              ALU.subtract).then_inc(sem("router_lo"), 1)

            def mixer(l, n):
                v = l + 1
                dve.memset(aug[:, :, 0:H, DH + 1:DH + 2], 1.0)
                dve.memset(aug[:, :, H:2 * H, DH:DH + 1], 1.0)
                step(n)
                step(n + 1)
                r = head_scales(f"fqk{l}", sq_early[:, :, :], DH, 2 * H, row_scale)
                then(dve.tensor_scalar(r[:, :, 0:H], r[:, :, 0:H], SCALE, None, ALU.mult))
                by_head(aug[:, :, :, 0:DH], ps[:, 0:2, :], r, DH).then_inc(sem("fqk_rows"), 1)
                z, az = (st[:, a:a + 8] for a in (72, 80))
                pair = lambda t: t.rearrange("p (b h) -> p b h", b=NB)
                used(dve, n + 2)
                for b in range(NB):
                    then(dve.scalar_tensor_tensor(out=z[:, b * H:(b + 1) * H], in0=ps[:, 2 + b, QK:QK + H],
                                                  scalar=row_scale[:, b:b + 1], in1=prm[:, BIAS + H * l:BIAS + H * (l + 1)],
                                                  op0=ALU.mult, op1=ALU.add))
                dve.scalar_tensor_tensor(out=az, in0=z, scalar=-1.0, in1=z, op0=ALU.mult, op1=ALU.max).then_inc(sem("z_ready"), 1)
                by_row(fval, ps[:, 2:4, 0:QK], row_scale).then_inc(sem("fv_copied"), 1)
                step(n + 2)
                dve.wait_ge(sem("ln_done"), v)
                dve.scalar_tensor_tensor(out=st[:, 64:72], in0=z, scalar=0.0, in1=st[:, 96:104], op0=ALU.min,
                                         op1=ALU.subtract).then_inc(sem("logf"), 1)
                step(n + 3)
                r = head_scales(f"mq{l}", sq_early[:, :, 0:QK], DH, H, row_scale)
                by_head(ymem, ps[:, 6:8, 0:QK], r, DH).then_inc(sem("mq_rows"), 1)
                step(n + 4)
                step(n + 5)
                dve.wait_ge(sem("logf_summed"), v)
                sums = ps[:, 4, 0:8].rearrange("p (b h) -> p b h", b=NB).unsqueeze(3)
                dve.tensor_copy(aug[:, :, 0:H, DH:DH + 1], sums)
                dve.tensor_scalar(aug[:, :, H:2 * H, DH + 1:DH + 2], sums, -1.0, None, ALU.mult).then_inc(sem("aug_ready"), 1)
                by_row(rot[:, 0], cos, row_scale)
                then(by_row(rot[:, 1], sin, row_scale))
                src = ps[:, 2:4, :].rearrange("p b (h c i) -> p b h c i", c=2, i=32)
                dst = rqk.rearrange("p b (h c i) -> p b h c i", c=2, i=32)
                cs, sn = (t.unsqueeze(2).to_broadcast([P, NB, 8, 32]) for t in (rot[:, 0], rot[:, 1]))
                for c, op in ((0, ALU.subtract), (1, ALU.add)):
                    tmp = sq_early[:, :, c * QK:(c + 1) * QK].rearrange("p b (h i) -> p b h i", i=32)
                    dve.tensor_tensor(dst[:, :, :, c, :], src[:, :, :, c, :], cs, ALU.mult)
                    then(dve.tensor_tensor(tmp, src[:, :, :, 1 - c, :], sn, ALU.mult))
                    last = dve.tensor_tensor(dst[:, :, :, c, :], dst[:, :, :, c, :], tmp, op)
                last.then_inc(sem("r_rotated"), 1)
                step(n + 6)
                dve.wait_ge(sem("f_turned"), v)
                dve.tensor_scalar(flat(fT[0:66, 0:H, :]), flat(ps[0:66, 4:6, :]), prm[0:66, G_FQ + l:G_FQ + l + 1], None,
                                  ALU.mult).then_inc(sem("f_T"), 1)

                def maxima(b, src, at, scored, done):
                    dve.wait_ge(sem(scored), NB * l + b + 1)
                    c = at + b * H
                    dve.tensor_reduce(st[:, c:c + H], src, AX.X, ALU.max, negate=True).then_inc(sem(done), 1)

                maxima(0, ps[:, 4, :].rearrange("p (h k) -> p h k", h=H), 32, "f_scored", "f_max")
                maxima(1, ps[:, 5:7, :].rearrange("p c (h k) -> p (c h) k", h=2), 32, "f_scored", "f_max")
                dve.wait_ge(sem("mq_turned"), v)
                dve.tensor_scalar(flat(mqT), ps[:, 7, :], prm[:, G_MQ + l:G_MQ + l + 1], SCALE, ALU.mult, ALU.mult)\
                    .then_inc(sem("mq_T"), 1)
                if l == 0:
                    memory_keys()
                step(n + 7)
                step(n + 8)
                if l == 0:
                    memory_turned()
                dve.wait_ge(sem("f_pturned"), NB * l + 2)
                dve.tensor_copy(flat(fpT1), flat(ps[:, 5:7, :])).then_inc(sem("f_pT"), 1)
                maxima(0, ps[:, 2:4, :].rearrange("p c (h k) -> p (c h) k", h=2), 48, "m_scored", "m_max")

                def weigh(dst, bank, at):
                    s, r = (st[:, a:a + 8].rearrange("p (b h) -> p b h", b=NB) for a in (at + 8, 112))
                    then(dve.reciprocal(r, s))
                    return by_head(dst, ps[:, bank, :].rearrange("p (b d) -> p b d", b=NB), r, DH)

                dve.wait_ge(sem("r_scored"), 2 * l + 1)
                dve.wait_ge(sem("f_valued"), v)
                dve.tensor_tensor(flat(rpT0), flat(ps[:, 0:2, :]), flat(decay), ALU.mult).then_inc(sem("r_decayed"), 1)
                weigh(yfox, 7, 32 + 0).then_inc(sem("f_out"), 1)
                maxima(1, ps[:, 4:6, :].rearrange("p c (h k) -> p (c h) k", h=2), 48, "m_scored", "m_max")
                dve.wait_ge(sem("r_scored"), 2 * l + 2)
                dve.tensor_tensor(rpT1.rearrange("p (c h) i -> p c h i", c=2),
                                  ps[:, 6:8, 0:2 * P].rearrange("p c (h i) -> p c h i", h=2),
                                  decay[:, :, 0:P].rearrange("p (c h) i -> p c h i", c=2), ALU.mult).then_inc(sem("r_decayed"), 1)
                r = head_scales(f"fo{l}", scaled[:, :, 0:QK], DH, H)
                by_head(yfox, yfox, r, DH)
                step(n + 9)
                r = head_scales(f"ro{l}", scaled[:, :, :], RDV, RH)
                then(by_head(rqk, ps[:, 0:2, :], r, RDV))
                for b in range(NB):
                    dve.tensor_tensor(yret[:, b], yret[:, b], rqk[:, b, :], ALU.mult).then_inc(sem("ret_rows"), 1)
                turn(f"out{l}", (0, 1))
                dve.wait_ge(sem("m_valued"), v)
                ins = weigh_mem(ps[:, 6, :])
                ins.then_inc(sem("m_out"), 1)
                r = head_scales(f"mo{l}", scaled[:, :, 0:QK], DH, H)
                for b in range(NB):
                    dve.tensor_tensor(ymem[:, b, :].rearrange("p (h d) -> p h d", d=DH),
                                      ymem[:, b, :].rearrange("p (h d) -> p h d", d=DH),
                                      r[:, b, :].unsqueeze(2).to_broadcast([P, H, DH]), ALU.mult)\
                        .then_inc(sem("mem_rows"), 1)
                turn(f"out{l}", (2, 3))
                for q in range(3):
                    step(n + 10 + q)
                next_turn(f"ffn{l}", n + 13, 0)

            def weigh_mem(src):
                s = st[:, 56:64].rearrange("p (b c h) -> p b h c", b=NB, c=2)
                r = st[:, 112:120].rearrange("p (b h c) -> p b h c", b=NB, c=2)
                then(dve.reciprocal(r, s))
                return by_head(ymem, src.rearrange("p (b d) -> p b d", b=NB),
                               st[:, 112:120].rearrange("p (b h) -> p b h", b=NB), DH)

            def hidden(it, c, nb, bank, unit):
                for b in range(nb):
                    dve.wait_ge(sem("silu_done"), counted(unit + b + 1, it, 2 * NCH))
                    if unit + b >= nb:
                        dve.wait_ge(sem("hid_turned"), counted(unit + b - nb + 1, it, 2 * NCH))
                    up = ps[:, bank + b, 0:CH[c]]
                    if nb > 1:
                        hidden = dve.scalar_tensor_tensor(out=hid[:, b, 0:CH[c]], in0=up, scalar=row_scale[:, b:b + 1],
                                                          in1=sil[:, b, 0:CH[c]], op0=ALU.mult, op1=ALU.mult)
                    else:
                        hidden = dve.tensor_tensor(hid[:, b, 0:CH[c]], up, sil[:, b, 0:CH[c]], ALU.mult)
                    hidden.then_inc(sem("hidden_ready"), 1)

            def hidden_lo(it, c, nb, bank, unit):
                for b in range(nb):
                    dve.wait_ge(sem("hid_hi"), counted(unit + b + 1, it, 2 * NCH))
                    full, rest = CH[c] // P, CH[c] % P
                    last = dve.tensor_tensor(flat(hidlo[:, b, 0:full, :]), ps[:, bank + b, 0:full * P],
                                             flat(hidhi[:, b, 0:full, :]).bitcast(F32), ALU.subtract)
                    if rest:
                        last = dve.tensor_tensor(hidlo[0:rest, b, full, :], ps[0:rest, bank + b, full * P:(full + 1) * P],
                                                 hidhi[0:rest, b, full, :].bitcast(F32), ALU.subtract)
                    last.then_inc(sem("hid_lo"), 1)

            mixer(0, IN0)
            n = DENSE0
            for c in range(NCH):
                step(n)
                if c:
                    hidden_lo(0, c - 1, NB, 2, NB * (c - 1))
                step(n + 1)
                rest = 4 if 0 < c < NCH - 1 else 2
                n += 2 + rest
                for i in range(rest):
                    if i == rest - 1:
                        used(dve, n - 1)
                        hidden(0, c, NB, 2, NB * c)
                    step(n - rest + i)
            step(n)
            hidden_lo(0, NCH - 1, NB, 2, NB * (NCH - 1))
            step(n + 1)
            n += 2
            next_turn("att1", n + 1, 4, n)
            mixer(1, IN1)
            dve.wait_ge(sem("logits"), 1)
            lg = st[:, 0:NB * E_].rearrange("p (b e) -> p b e", b=NB)
            then(by_row(lg, ps[:, 1, 0:NB * E_].rearrange("p (b e) -> p b e", b=NB), row_scale))
            for b in range(NB):
                last = dve.max(mx[:, b, :], lg[:, b, :])
            then(last)
            for b in range(NB):
                last = dve.max_index(mi[:, b, :], mx[:, b, :], lg[:, b, :])
            then(last)
            then(dve.tensor_copy(mif[:, :, :], mi[:, :, :]))
            dve.tensor_tensor(st[:, 106:108].unsqueeze(2), mx[:, :, 1:2], mx[:, :, 0:1], ALU.subtract)\
                .then_inc(sem("top_two"), 1)
            iota = tb[:, T_IOTA:T_IOTA + P]
            for b in range(NB):
                last = dve.tensor_scalar(sel[:, b, :], iota[:, 0:E_], mif[:, b, 0:1], None, ALU.is_equal)
            then(last)
            for b in range(NB):
                last = dve.scalar_tensor_tensor(out=sel[:, b, :], in0=iota[:, 0:E_], scalar=mif[:, b, 1:2],
                                                in1=sel[:, b, :], op0=ALU.is_equal, op1=ALU.add)
            last.then_inc(sem("chosen"), 1)
            then(dve.memset(slot_of[:, :, :], -1.0))
            dve.wait_ge(sem("rows_hi"), 1)
            for b in range(NB):
                last = dve.scalar_tensor_tensor(out=toklo[:, b, :], in0=xres[:, b, :], scalar=row_scale[:, b:b + 1],
                                                in1=tokhi[:, b, :].bitcast(F32), op0=ALU.mult, op1=ALU.subtract)
            last.then_inc(sem("rows_split"), 1)
            dve.wait_ge(sem("ranked"), 1)
            upto = ps[:, 7, 0:NB * E_].rearrange("p (b e) -> p b e", b=NB)
            then(dve.tensor_tensor(slot_of[:, :, 0:E_], upto, sel[:, :, :], ALU.mult))
            then(dve.tensor_scalar(slot_of[:, :, 0:E_], slot_of[:, :, 0:E_], -1.0, None, ALU.add))
            def onehot_in(k, it):
                if k:
                    dve.wait_ge(sem("collected"), counted(2 * k, it, 4))
                for b in range(NB):
                    col = slot_of[:, b, k:k + 1] if isinstance(it, int) else slot_of[:, b, bass.ds(it * 2 + k, 1)]
                    last = dve.tensor_scalar(onehot[:, b, :], iota, col, None, ALU.is_equal)
                last.then_inc(sem("onehot_ready"), 1)

            onehot_in(0, 0)
            then(dve.tensor_scalar(slot_of[:, :, E_:2 * E_], slot_of[:, :, 0:E_], float(-P), None, ALU.add))
            then(dve.tensor_reduce(st[:, 126:127], ps[:, 7, NB * E_:(NB + 1) * E_], AX.X, ALU.max))
            then(dve.tensor_scalar(flag[:, :], st[:, 126:127], float(P), None, ALU.is_gt))
            dve.memset(st[:, 127:128], 0.0).then_inc(sem("flag_ready"), 1)

            dve.wait_ge(sem("gate_exp"), 1)
            g0, g1, den = st[:, 120:122], st[:, 122:124], st[:, 124:126]
            then(dve.tensor_scalar(den, st[:, 108:110], 1.0, None, ALU.add))
            then(dve.reciprocal(g0, den))
            then(dve.tensor_tensor(g1, g0, st[:, 108:110], ALU.mult))
            for b in range(NB):
                then(dve.tensor_scalar(comb[:, b, :], iota[:, 0:E_], mif[:, b, 0:1], g0[:, b:b + 1], ALU.is_equal, ALU.mult))
                then(dve.tensor_scalar(st[:, 40:48], iota[:, 0:E_], mif[:, b, 1:2], g1[:, b:b + 1], ALU.is_equal, ALU.mult))
                then(dve.tensor_tensor(comb[:, b, :], comb[:, b, :], st[:, 40:48], ALU.add))
            step(MOE0 - 1)

            def gathered_scale(k, it, half, bank=3):
                dve.wait_ge(sem("gathered"), counted(2 * k + half + 1, it, 4))
                if k:
                    dve.wait_ge(sem("gathered_lo"), counted(2 * k + half - 1, it, 4))
                else:
                    dve.wait_ge(sem("turn_lo"), 4 * len(TURNS))
                scale_unit(ps[:, bank, :], GAIN["ffn1"], half, scaled[:, half, :], "gathered_scaled")

            def gathered_rest(k, it, par, half):
                dve.wait_ge(sem("gathered_hi"), counted(2 * k + half + 1, it, 4))
                dve.tensor_tensor(flat(stlo[:, par, 4 * half:4 * half + 4, :]), scaled[:, half, :],
                                  flat(sthi[:, par, 4 * half:4 * half + 4, :]).bitcast(F32), ALU.subtract)\
                    .then_inc(sem("gathered_lo"), 1)

            def out_rest(k, it):
                dve.wait_ge(sem("out_hi"), counted(k + 1, it, 2))
                dve.tensor_tensor(outlo[:, :], flat(ps[:, 4:6, :]), outhi[:, :].bitcast(F32), ALU.subtract).then_inc(sem("out_copied"), 1)

            def scatter_add(k, e, it, b, banks=6):
                dve.wait_ge(sem("scattered"), counted(2 * k + b + 1, it, 4))
                gate = comb[:, b, e:e + 1] if isinstance(it, int) else comb[:, b, bass.ds(it * 2 + e, 1)]
                if k or b or not isinstance(it, int):
                    dve.wait_ge(sem("scatter_added"), counted(2 * k + b, it, 4))
                dve.scalar_tensor_tensor(out=xres[:, b, :], in0=flat(ps[:, banks:banks + 2, :]), scalar=gate, in1=xres[:, b, :],
                                         op0=ALU.mult, op1=ALU.add).then_inc(sem("scatter_added"), 1)

            def expert_pair(rnd, it):
                def after(par, c, what, n):
                    k = rnd * E_ + par
                    u = DENSE_UNITS + k * NCH + c
                    before = not (isinstance(it, int) and par == 0)
                    if what in (("gate", 1), ("up", 1)):
                        used(dve, n, it)
                    if what == ("gate", 1) and (c or before):
                        hidden_lo(it, (c - 1) % NCH, 1, 1, u - 1)
                    if what == ("up", 1):
                        hidden(it, c, 1, 2, u)
                    if what == ("gate", 1) and c == 1:
                        onehot_in(k + 1, it)
                    if (c, what) in ((4, ("down", 0)), (5, ("gate", 1))):
                        gathered_scale(k + 1, it, c - 4)
                    if (c, what) in ((4, ("down", 1)), (5, ("up", 1))):
                        gathered_rest(k + 1, it, 1 - par, c - 4)
                    if what == ("down", 1) and c == 0:
                        out_rest(k - 1, it)
                    if what == ("down", 1) and c in (1, 2) and before:
                        scatter_add(k - 1, par - 1, it, c - 1)
                split_pair(split_lo, dve, rnd, it, after)

            def expert_round(rnd):
                expert_pair(rnd, 0)
                with dve.Fori(1, E_ // 2) as it:
                    expert_pair(rnd, it)
                n0 = MOE0 + (rnd + 1) * MOE_LOADS - 2
                for h in range(2):
                    split_lo(dve, n0 + h, FLUSH[h])
                hidden_lo(0, NCH - 1, 1, 1, DENSE_UNITS + (rnd + 1) * E_ * NCH - 1)
                k = (rnd + 1) * E_ - 1
                out_rest(k, 0)
                for b in range(NB):
                    scatter_add(k, E_ - 1, 0, b, (6, 2)[b])
                dve.wait_ge(sem("scatter_added"), 2 * (k + 1))

            for half in range(2):
                gathered_scale(0, 0, half, 3 - half)
                gathered_rest(0, 0, 0, half)
            expert_round(0)
            dve.wait_ge(sem("flag_ready"), 1)
            with dve.If(dve.value_load(flag[0:1, 0:1], min_val=0, max_val=1) > 0):
                expert_round(1)
            with dve.Else():
                dve.nop()


def tables():
    t = np.zeros((P, NTAB), np.float32)
    heads = np.arange(RH, dtype=np.float32)
    log_g = np.log1p(-np.exp2(-5.0 - heads)).astype(np.float64)
    j, i = np.arange(P)[:, None], np.arange(SEQ)[None, :]
    dec = t[:, T_DEC:T_DEC + 4 * SEQ].reshape(P, RH, SEQ)
    for h in range(RH):
        dec[:, HEAD_AT[h], :] = np.where(i >= j, np.exp(log_g[h] * np.maximum(i - j, 0)), 0.0) * SCALE
    t[:, T_DEC:T_DEC + 4 * SEQ] = dec.reshape(P, -1)
    pos = (np.arange(NB)[None, :, None] * P + np.arange(P)[:, None, None]).astype(np.float32)
    freq = (np.float32(10000.0) ** (-np.arange(32, dtype=np.float32) / np.float32(32))).astype(np.float32)
    ang = (pos * freq[None, None, :]).astype(np.float32).astype(np.float64)
    t[:, T_COS:T_COS + NB * 32] = np.cos(ang).reshape(P, -1)
    t[:, T_SIN:T_SIN + NB * 32] = np.sin(ang).reshape(P, -1)
    t[:, T_ID:T_ID + P] = np.eye(P)
    r, c = np.arange(P)[:, None], np.arange(P)[None, :]
    t[:, T_TRI:T_TRI + P] = r <= c
    t[:, T_ONE:T_ONE + P] = 1.0
    t[:, T_MASK:T_MASK + P] = np.where(c <= r, 0.0, NEG)
    t[:, T_IOTA:T_IOTA + P] = c
    return t


def parameters(a):
    p = np.zeros((P, NPAR), np.float32)
    for name, at in (("attn_norm_g", G_ATT), ("ffn_norm_g", G_FFN), ("out_norm_g", G_OUT), ("mem_norm_g", G_MEM)):
        for l in range(DEPTH):
            p[:, at + KT * l:at + KT * (l + 1)] = a[name][l].reshape(KT, P).T
    for name, at in (("fox_q_norm_g", G_FQ), ("fox_k_norm_g", G_FK)):
        for l in range(DEPTH):
            p[0:DH, at + l] = a[name][l]
            p[DH:DH + 2, at + l] = 1.0
    for name, at in (("mem_q_norm_g", G_MQ), ("mem_k_norm_g", G_MK)):
        for l in range(DEPTH):
            p[0:DH, at + l] = a[name][l]
            p[DH:2 * DH, at + l] = a[name][l]
    for l in range(DEPTH):
        p[:, BIAS + H * l:BIAS + H * (l + 1)] = a["forget_bias"][l][None, :]
    p[:, ROUT:ROUT + KT * E_] = a["router_w"][0].reshape(KT, P, E_).transpose(1, 0, 2).reshape(P, KT * E_)
    return p


_INS = ["x", "mem", "w_in", "w_mem_kv", "w_out", "dense_w_gate", "dense_w_up", "dense_w_down",
        "expert_w_gate", "expert_w_up", "expert_w_down"]


def kernel(**inputs):
    import concourse.bacc as bacc
    from concourse.bass_utils import run_bass_kernel_spmd

    nc = bacc.Bacc("TRN2", target_bir_lowering=False, num_devices=1, dynamic_dma_scratch_size=1024)
    host = {k: np.ascontiguousarray(np.asarray(v)) for k, v in inputs.items()}
    arrays = {f"in_{n}": host[n] for n in _INS}
    arrays["in_par"] = parameters(host)
    arrays["in_tab"] = tables()
    args = [nc.dram_tensor(n, a.shape, F32, kind="ExternalInput").ap() for n, a in arrays.items()]
    args.append(nc.dram_tensor("out_x", (1, SEQ, D), F32, kind="ExternalOutput").ap())
    build(nc, *args)
    r = run_bass_kernel_spmd(nc, [arrays], core_ids=[0])
    return r.results[0]["out_x"]
```
